# Optimizing a Trainium2 kernel written in Bass

```python
import math
import jax, jax.numpy as jnp
from jax import lax
import numpy as np

D_MODEL = 1024
BATCH = 1
SEQ = 512
DEPTH = 1

D_RNN = D_MODEL
RNN_HEADS = 8
RNN_BLOCK = D_RNN // RNN_HEADS
RNN_CONV = 4
RG_C = 8.0
ATT_HEADS = 8
HEAD_DIM = 128
ATT_WIDTH = ATT_HEADS * HEAD_DIM
Q_BLOCK = 128
D_FF = 3 * D_MODEL
FFN_CONV = 3
EPS = 1e-6
IN_SPLITS = (D_RNN, D_RNN, ATT_WIDTH, ATT_WIDTH, ATT_WIDTH, D_MODEL, D_MODEL)
D_IN = sum(IN_SPLITS)


def rmsnorm(x, g):
    x32 = x.astype(jnp.float32)
    y = x32 * lax.rsqrt(jnp.mean(x32 * x32, axis=-1, keepdims=True) + EPS)
    return (y * g.astype(jnp.float32)).astype(x.dtype)

def causal_dwconv(x, w, b):
    k_w = w.shape[0]
    s = x.shape[1]
    xp = jnp.pad(x, ((0, 0), (k_w - 1, 0), (0, 0)))
    out = b + w[0] * xp[:, 0:s]
    for k in range(1, k_w):
        out = out + w[k] * xp[:, k:k + s]
    return out

def rg_lru(x, wa, ba, wx, bx, lam):
    b_, s_, c_ = x.shape
    xh = x.reshape(b_, s_, RNN_HEADS, RNN_BLOCK)
    r = jax.nn.sigmoid(jnp.einsum('bshi,hij->bshj', xh, wa).reshape(b_, s_, c_) + ba)
    i = jax.nn.sigmoid(jnp.einsum('bshi,hij->bshj', xh, wx).reshape(b_, s_, c_) + bx)
    log_a = -RG_C * r.astype(jnp.float32) * jax.nn.softplus(-lam.astype(jnp.float32))
    a = jnp.exp(log_a)
    mult = jnp.sqrt(-jnp.expm1(2.0 * log_a))
    u = mult * (i * x).astype(jnp.float32)

    def step(h, inp):
        a_t, u_t = inp
        h = a_t * h + u_t
        return h, h

    h0 = jnp.zeros((b_, c_), jnp.float32)
    _, hs = lax.scan(step, h0, (jnp.swapaxes(a, 0, 1), jnp.swapaxes(u, 0, 1)))
    return jnp.swapaxes(hs, 0, 1).astype(x.dtype)

def head_rmsnorm(x, g):
    return rmsnorm(x, g)

def stick_breaking_attention(q, k, v):
    b_, s_, h_, d_ = q.shape
    nb = s_ // Q_BLOCK
    scale = 1.0 / math.sqrt(d_)
    kh = jnp.transpose(k, (0, 2, 1, 3))
    vh = jnp.transpose(v, (0, 2, 1, 3))
    qb = jnp.transpose(q.reshape(b_, nb, Q_BLOCK, h_, d_), (1, 0, 3, 2, 4))
    key_pos = jnp.arange(s_)

    def one_block(args):
        q_blk, blk = args
        q_pos = blk * Q_BLOCK + jnp.arange(Q_BLOCK)
        mask = key_pos[None, :] < q_pos[:, None]
        z = jnp.einsum('bhqd,bhkd->bhqk', q_blk, kh).astype(jnp.float32) * scale
        log_beta = jax.nn.log_sigmoid(z)
        log_1mb = jnp.where(mask, log_beta - z, 0.0)
        suffix = lax.cumsum(log_1mb, axis=3, reverse=True) - log_1mb
        attn = jnp.where(mask, jnp.exp(log_beta + suffix), 0.0)
        return jnp.einsum('bhqk,bhkd->bhqd', attn.astype(v.dtype), vh)

    out = lax.map(one_block, (qb, jnp.arange(nb)))
    return jnp.transpose(out, (1, 0, 3, 2, 4)).reshape(b_, s_, h_ * d_)

def first_inputs(seed: int = 0) -> dict:
    key = jax.random.key(seed)
    ks = jax.random.split(key, 24)
    n = jax.random.normal
    L, D = DEPTH, D_MODEL
    u = jax.random.uniform(ks[10], (L, D_RNN), minval=0.9, maxval=0.999)
    a0 = u ** (1.0 / RG_C)
    lam = jnp.log(a0) - jnp.log1p(-a0)
    return {
        "x": n(ks[0], (BATCH, SEQ, D), jnp.float32),
        "c": n(ks[1], (BATCH, D), jnp.float32),
        "ada_w": n(ks[2], (L, D, 6 * D), jnp.float32) * (0.5 * D ** -0.5),
        "ada_b": n(ks[3], (L, 6 * D), jnp.float32) * 0.01,
        "norm1_g": 1.0 + 0.05 * n(ks[4], (L, D), jnp.float32),
        "w_in": n(ks[5], (L, D, D_IN), jnp.float32) * D ** -0.5,
        "conv_w": n(ks[6], (L, RNN_CONV, D_RNN), jnp.float32) * RNN_CONV ** -0.5,
        "conv_b": n(ks[7], (L, D_RNN), jnp.float32) * 0.01,
        "rg_wa": n(ks[8], (L, RNN_HEADS, RNN_BLOCK, RNN_BLOCK), jnp.float32) * RNN_BLOCK ** -0.5,
        "rg_ba": n(ks[9], (L, D_RNN), jnp.float32) * 0.01,
        "rg_wx": n(ks[11], (L, RNN_HEADS, RNN_BLOCK, RNN_BLOCK), jnp.float32) * RNN_BLOCK ** -0.5,
        "rg_bx": n(ks[12], (L, D_RNN), jnp.float32) * 0.01,
        "rg_lambda": lam.astype(jnp.float32),
        "q_norm_g": 1.0 + 0.05 * n(ks[13], (L, HEAD_DIM), jnp.float32),
        "k_norm_g": 1.0 + 0.05 * n(ks[14], (L, HEAD_DIM), jnp.float32),
        "w_out": n(ks[15], (L, D, D), jnp.float32) * D ** -0.5,
        "norm2_g": 1.0 + 0.05 * n(ks[16], (L, D), jnp.float32),
        "ffn_up": n(ks[17], (L, D, 2 * D_FF), jnp.float32) * D ** -0.5,
        "ffn_conv_w": n(ks[18], (L, FFN_CONV, 2 * D_FF), jnp.float32) * FFN_CONV ** -0.5,
        "ffn_conv_b": n(ks[19], (L, 2 * D_FF), jnp.float32) * 0.01,
        "ffn_down": n(ks[20], (L, D_FF, D), jnp.float32) * D_FF ** -0.5,
    }

def first_block(x, c, ada_w, ada_b, norm1_g, w_in, conv_w, conv_b, rg_wa, rg_ba, rg_wx, rg_bx,
              rg_lambda, q_norm_g, k_norm_g, w_out, norm2_g, ffn_up, ffn_conv_w, ffn_conv_b,
              ffn_down):
    b_, s_, d_ = x.shape
    cuts = np.cumsum(IN_SPLITS)[:-1].tolist()
    for l in range(DEPTH):
        mod = c @ ada_w[l] + ada_b[l]
        sh1, sc1, gt1, sh2, sc2, gt2 = [m[:, None, :] for m in jnp.split(mod, 6, axis=-1)]

        h = rmsnorm(x, norm1_g[l]) * (1.0 + sc1) + sh1
        p = h @ w_in[l]
        xr, yr, q, k, v, ga, gb = jnp.split(p, cuts, axis=-1)

        xr = causal_dwconv(xr, conv_w[l], conv_b[l])
        y_a = rg_lru(xr, rg_wa[l], rg_ba[l], rg_wx[l], rg_bx[l], rg_lambda[l]) * jax.nn.gelu(yr)

        q = head_rmsnorm(q.reshape(b_, s_, ATT_HEADS, HEAD_DIM), q_norm_g[l])
        k = head_rmsnorm(k.reshape(b_, s_, ATT_HEADS, HEAD_DIM), k_norm_g[l])
        v = v.reshape(b_, s_, ATT_HEADS, HEAD_DIM)
        y_b = stick_breaking_attention(q, k, v)

        mix = jax.nn.sigmoid(ga) * y_a + jax.nn.sigmoid(gb) * y_b
        x = x + gt1 * (mix @ w_out[l])

        h2 = rmsnorm(x, norm2_g[l]) * (1.0 + sc2) + sh2
        up = causal_dwconv(h2 @ ffn_up[l], ffn_conv_w[l], ffn_conv_b[l])
        g_ff, v_ff = jnp.split(up, 2, axis=-1)
        x = x + gt2 * ((jax.nn.gelu(g_ff) * v_ff) @ ffn_down[l])
    return x


DEPTH_2 = 2

ROPE_BASE = 10000.0
NORM_EPS = 1e-6
MLA_HEADS = D_MODEL // 128
MLA_QK_NOPE = 128
MLA_QK_ROPE = 64
MLA_V_DIM = 128
MLA_Q_LORA = 3 * D_MODEL // 8
MLA_KV_LORA = D_MODEL // 8
ATTN_Q_BLOCK = 128
POOL_WINDOWS = (2, 4, 8, 16)
POOL_GROUPS = len(POOL_WINDOWS)
POOL_GROUP_DIM = D_MODEL // POOL_GROUPS
MIX_A = MLA_HEADS * MLA_V_DIM
MIX_B = POOL_GROUPS * POOL_GROUP_DIM
EVEN_MIX = MIX_A + MIX_B
EVEN_SPLITS = (MLA_Q_LORA, MLA_Q_LORA + MLA_KV_LORA, MLA_Q_LORA + MLA_KV_LORA + MLA_QK_ROPE,
               MLA_Q_LORA + MLA_KV_LORA + MLA_QK_ROPE + MIX_B)
EVEN_IN = EVEN_SPLITS[-1] + EVEN_MIX
RET_HEADS = D_MODEL // 256
RET_DK = 256
RET_DV = 512
RET_CHUNK = 128
RET_QK = RET_HEADS * RET_DK
RET_V = RET_HEADS * RET_DV
ODD_IN = 2 * RET_QK + 2 * RET_V
N_EVEN = (DEPTH_2 + 1) // 2
N_ODD = DEPTH_2 // 2


def rms_norm(x, g):
    xf = x.astype(jnp.float32)
    y = xf * lax.rsqrt(jnp.mean(xf * xf, axis=-1, keepdims=True) + NORM_EPS)
    return (y * g.astype(jnp.float32)).astype(x.dtype)

def rope_tables(positions, dim):
    inv = 1.0 / (ROPE_BASE ** (jnp.arange(0, dim, 2, dtype=jnp.float32) / dim))
    ang = positions.astype(jnp.float32)[..., None] * inv
    return jnp.cos(ang)[:, :, None, :], jnp.sin(ang)[:, :, None, :]

def apply_rope(x, cos, sin):
    half = x.shape[-1] // 2
    xf = x.astype(jnp.float32)
    x1, x2 = xf[..., :half], xf[..., half:]
    return jnp.concatenate([x1 * cos - x2 * sin, x2 * cos + x1 * sin], axis=-1).astype(x.dtype)

def mla(cq, ckv, kr, cos, sin, q_norm_g, w_uq, kv_norm_g, w_ukv):
    B_, T, _ = cq.shape
    dqk = MLA_QK_NOPE + MLA_QK_ROPE
    q = (rms_norm(cq, q_norm_g) @ w_uq).reshape(B_, T, MLA_HEADS, dqk)
    q = jnp.concatenate([q[..., :MLA_QK_NOPE], apply_rope(q[..., MLA_QK_NOPE:], cos, sin)], axis=-1)
    kv = (rms_norm(ckv, kv_norm_g) @ w_ukv).reshape(B_, T, MLA_HEADS, MLA_QK_NOPE + MLA_V_DIM)
    k_rope = apply_rope(kr[:, :, None, :], cos, sin)
    k = jnp.concatenate([kv[..., :MLA_QK_NOPE],
                         jnp.broadcast_to(k_rope, (B_, T, MLA_HEADS, MLA_QK_ROPE))], axis=-1)
    v = kv[..., MLA_QK_NOPE:]
    nb = T // ATTN_Q_BLOCK
    qb = q.reshape(B_, nb, ATTN_Q_BLOCK, MLA_HEADS, dqk).transpose(1, 0, 2, 3, 4)
    scale = dqk ** -0.5

    def attend(q_blk):
        s = jnp.einsum('bqhd,bkhd->bhqk', q_blk, k, preferred_element_type=jnp.float32) * scale
        p = jax.nn.softmax(s, axis=-1).astype(v.dtype)
        return jnp.einsum('bhqk,bkhd->bqhd', p, v)

    o = lax.map(attend, qb)
    return o.transpose(1, 0, 2, 3, 4).reshape(B_, T, MIX_A)

def multiscale_pool(u, pool_w, pool_scale):
    B_, T, _ = u.shape
    uf = u.reshape(B_, T, POOL_GROUPS, POOL_GROUP_DIM).astype(jnp.float32)
    cs = jnp.concatenate([jnp.zeros_like(uf[:, :1]), jnp.cumsum(uf, axis=1)], axis=1)
    t = jnp.arange(T)
    outs = []
    for g, w in enumerate(POOL_WINDOWS):
        left = w // 2
        right = w - 1 - left
        lo = jnp.clip(t - left, 0, T - 1)
        hi = jnp.clip(t + right, 0, T - 1)
        csg = cs[:, :, g]
        s = jnp.take(csg, hi + 1, axis=1) - jnp.take(csg, lo, axis=1)
        cnt = (hi - lo + 1).astype(jnp.float32)
        outs.append(s / cnt[None, :, None] - uf[:, :, g])
    d = jnp.stack(outs, axis=2).astype(u.dtype)
    y = jnp.einsum('btgc,gcd->btgd', d, pool_w) * pool_scale.reshape(POOL_GROUPS, POOL_GROUP_DIM)
    return y.reshape(B_, T, MIX_B)

def hybrid_attn_pool_layer(x, cos_a, sin_a, norm_g, w_in, q_norm_g, w_uq, kv_norm_g, w_ukv,
                           pool_w, pool_scale, w_out):
    h = rms_norm(x, norm_g)
    proj = h @ w_in
    cq, ckv, kr, u, gate = jnp.split(proj, list(EVEN_SPLITS), axis=-1)
    a = mla(cq, ckv, kr, cos_a, sin_a, q_norm_g, w_uq, kv_norm_g, w_ukv)
    b = multiscale_pool(u, pool_w, pool_scale)
    y = jnp.concatenate([a, b], axis=-1) * jax.nn.silu(gate)
    return y @ w_out

def retention_chunkwise(q, k, v, log_g, include_diag):
    B_, T, H, dk = q.shape
    dv = v.shape[-1]
    C = RET_CHUNK
    N = T // C
    to_chunks = lambda a: a.reshape(B_, N, C, H, a.shape[-1]).transpose(1, 0, 3, 2, 4)
    qc, kc, vc = to_chunks(q), to_chunks(k), to_chunks(v)
    idx = jnp.arange(C).astype(jnp.float32)
    diff = idx[:, None] - idx[None, :]
    mask = (diff >= 0) if include_diag else (diff > 0)
    dmat = jnp.where(mask[None], jnp.exp(jnp.where(mask, diff, 0.0)[None] * log_g[:, None, None]), 0.0)
    xi = jnp.exp((idx + 1.0)[None, :] * log_g[:, None])[None, :, :, None]
    zeta = jnp.exp((C - 1.0 - idx)[None, :] * log_g[:, None])[None, :, :, None]
    chunk_decay = jnp.exp(C * log_g)[None, :, None, None]

    def step(state, inp):
        q_i, k_i, v_i = inp
        scores = jnp.einsum('bhid,bhjd->bhij', q_i, k_i) * dmat
        o_in = jnp.einsum('bhij,bhjv->bhiv', scores, v_i)
        o_cross = jnp.einsum('bhid,bhdv->bhiv', q_i, state) * xi
        state = state * chunk_decay + jnp.einsum('bhjd,bhjv->bhdv', k_i * zeta, v_i)
        return state, o_in + o_cross

    s0 = jnp.zeros((B_, H, dk, dv), jnp.float32)
    _, o = lax.scan(step, s0, (qc, kc, vc))
    return o.transpose(1, 0, 3, 2, 4).reshape(B_, T, H, dv)

def retention_layer(x, cos_r, sin_r, norm_g, w_in, decay_fwd, decay_bwd, gn_g, w_out):
    B_, T, _ = x.shape
    h = rms_norm(x, norm_g)
    proj = h @ w_in
    q, k, v, gate = jnp.split(proj, [RET_QK, 2 * RET_QK, 2 * RET_QK + RET_V], axis=-1)
    q = apply_rope(q.reshape(B_, T, RET_HEADS, RET_DK), cos_r, sin_r).astype(jnp.float32)
    k = apply_rope(k.reshape(B_, T, RET_HEADS, RET_DK), cos_r, sin_r).astype(jnp.float32) * (RET_DK ** -0.5)
    v = v.reshape(B_, T, RET_HEADS, RET_DV).astype(jnp.float32)
    lf = jax.nn.log_sigmoid(decay_fwd.astype(jnp.float32))
    lb = jax.nn.log_sigmoid(decay_bwd.astype(jnp.float32))
    o_f = retention_chunkwise(q, k, v, lf, True)
    o_b = jnp.flip(retention_chunkwise(jnp.flip(q, 1), jnp.flip(k, 1), jnp.flip(v, 1), lb, False), 1)
    o = o_f + o_b
    mu = jnp.mean(o, axis=-1, keepdims=True)
    var = jnp.mean(jnp.square(o - mu), axis=-1, keepdims=True)
    o = ((o - mu) * lax.rsqrt(var + NORM_EPS)).reshape(B_, T, RET_V) * gn_g.astype(jnp.float32)
    y = o.astype(x.dtype) * jax.nn.silu(gate)
    return y @ w_out

def second_inputs(seed: int = 0) -> dict:
    key = jax.random.key(seed)
    ks = jax.random.split(key, 24)
    f32 = jnp.float32
    nrm = lambda k, shape, scale: jax.random.normal(k, shape, f32) * scale
    gain = lambda k, shape: 1.0 + 0.05 * jax.random.normal(k, shape, f32)
    x = jax.random.normal(ks[0], (BATCH, SEQ, D_MODEL), f32)
    positions = (jnp.arange(SEQ, dtype=jnp.int32)[None, :]
                 + jax.random.randint(ks[1], (BATCH, 1), 0, 4096, dtype=jnp.int32))
    base_decay = jnp.log(2.0 ** (5.0 + jnp.arange(RET_HEADS, dtype=f32)) - 1.0)
    return {
        'x': x,
        'positions': positions,
        'a_norm_g': gain(ks[2], (N_EVEN, D_MODEL)),
        'a_w_in': nrm(ks[3], (N_EVEN, D_MODEL, EVEN_IN), D_MODEL ** -0.5),
        'a_q_norm_g': gain(ks[4], (N_EVEN, MLA_Q_LORA)),
        'a_w_uq': nrm(ks[5], (N_EVEN, MLA_Q_LORA, MLA_HEADS * (MLA_QK_NOPE + MLA_QK_ROPE)), MLA_Q_LORA ** -0.5),
        'a_kv_norm_g': gain(ks[6], (N_EVEN, MLA_KV_LORA)),
        'a_w_ukv': nrm(ks[7], (N_EVEN, MLA_KV_LORA, MLA_HEADS * (MLA_QK_NOPE + MLA_V_DIM)), MLA_KV_LORA ** -0.5),
        'a_pool_w': nrm(ks[8], (N_EVEN, POOL_GROUPS, POOL_GROUP_DIM, POOL_GROUP_DIM), POOL_GROUP_DIM ** -0.5),
        'a_pool_scale': 1.0 + 0.1 * jax.random.normal(ks[9], (N_EVEN, MIX_B), f32),
        'a_w_out': nrm(ks[10], (N_EVEN, EVEN_MIX, D_MODEL), EVEN_MIX ** -0.5),
        'r_norm_g': gain(ks[11], (N_ODD, D_MODEL)),
        'r_w_in': nrm(ks[12], (N_ODD, D_MODEL, ODD_IN), D_MODEL ** -0.5),
        'r_decay_fwd': base_decay[None, :] + 0.1 * jax.random.normal(ks[13], (N_ODD, RET_HEADS), f32),
        'r_decay_bwd': base_decay[None, :] + 0.1 * jax.random.normal(ks[14], (N_ODD, RET_HEADS), f32),
        'r_gn_g': gain(ks[15], (N_ODD, RET_V)),
        'r_w_out': nrm(ks[16], (N_ODD, RET_V, D_MODEL), RET_V ** -0.5),
        'final_norm_g': gain(ks[17], (D_MODEL,)),
    }

def second_block(x, positions, a_norm_g, a_w_in, a_q_norm_g, a_w_uq, a_kv_norm_g, a_w_ukv,
              a_pool_w, a_pool_scale, a_w_out, r_norm_g, r_w_in, r_decay_fwd, r_decay_bwd,
              r_gn_g, r_w_out, final_norm_g):
    cos_a, sin_a = rope_tables(positions, MLA_QK_ROPE)
    cos_r, sin_r = rope_tables(positions, RET_DK)
    for layer in range(DEPTH_2):
        i = layer // 2
        if layer % 2 == 0:
            x = x + hybrid_attn_pool_layer(x, cos_a, sin_a, a_norm_g[i], a_w_in[i], a_q_norm_g[i],
                                           a_w_uq[i], a_kv_norm_g[i], a_w_ukv[i], a_pool_w[i],
                                           a_pool_scale[i], a_w_out[i])
        else:
            x = x + retention_layer(x, cos_r, sin_r, r_norm_g[i], r_w_in[i], r_decay_fwd[i],
                                    r_decay_bwd[i], r_gn_g[i], r_w_out[i])
    return rms_norm(x, final_norm_g)


def setup_inputs(seed=0):
    out = dict(first_inputs(seed))
    for name, value in second_inputs(seed + 1).items():
        if name != "x":
            out[name + "_2"] = value
    return out


def reference(
    x, c, ada_w, ada_b, norm1_g, w_in, conv_w, conv_b, rg_wa, rg_ba, rg_wx, rg_bx, rg_lambda,
    q_norm_g, k_norm_g, w_out, norm2_g, ffn_up, ffn_conv_w, ffn_conv_b, ffn_down, positions_2,
    a_norm_g_2, a_w_in_2, a_q_norm_g_2, a_w_uq_2, a_kv_norm_g_2, a_w_ukv_2, a_pool_w_2,
    a_pool_scale_2, a_w_out_2, r_norm_g_2, r_w_in_2, r_decay_fwd_2, r_decay_bwd_2, r_gn_g_2,
    r_w_out_2, final_norm_g_2,
):
    x = first_block(
        x, c, ada_w, ada_b, norm1_g, w_in, conv_w, conv_b, rg_wa, rg_ba, rg_wx, rg_bx,
        rg_lambda, q_norm_g, k_norm_g, w_out, norm2_g, ffn_up, ffn_conv_w, ffn_conv_b, ffn_down,
    )
    return second_block(
        x, positions_2, a_norm_g_2, a_w_in_2, a_q_norm_g_2, a_w_uq_2, a_kv_norm_g_2, a_w_ukv_2,
        a_pool_w_2, a_pool_scale_2, a_w_out_2, r_norm_g_2, r_w_in_2, r_decay_fwd_2,
        r_decay_bwd_2, r_gn_g_2, r_w_out_2, final_norm_g_2,
    )


_drawn_inputs = setup_inputs


def setup_inputs(seed=0):
    import zlib

    import numpy as np

    out = dict(_drawn_inputs(seed))
    spreads = {}
    factors = {'conv_b': 4.577,
     'rg_ba': 8.0,
     'rg_bx': 8.0,
     'q_norm_g': 8.0,
     'k_norm_g': 8.0,
     'ffn_conv_b': 8.0,
     'a_q_norm_g_2': 8.0,
     'a_kv_norm_g_2': 8.0,
     'r_gn_g_2': 7.676,
     'a_pool_scale_2': 4.379}
    for name, (base, spread) in spreads.items():
        noise = np.random.default_rng([zlib.crc32(name.encode()), seed]).standard_normal(out[name].shape)
        drawn = base * np.exp(spread * noise) if base else spread * noise
        out[name] = __import__('jax').numpy.asarray(drawn.astype(out[name].dtype))
    for name, factor in factors.items():
        out[name] = (out[name] * factor).astype(out[name].dtype)
    return out
```

```python
from contextlib import ExitStack

import numpy as np

import concourse.bass as bass
from concourse import mybir

P = 128
T = 512
D = 1024
DK = D // P
HEADS = 8
TB = T // P
D_FF = 3072
THIRDS = 3
RH = 4
RDK = 256
RDV = 512
EPS = 1e-6
RG_C = 8.0
NR = 3
AHEAD = 2

F32 = mybir.dt.float32
F32R = mybir.dt.float32r
I32 = mybir.dt.int32
ALU = mybir.AluOpType
ACT = mybir.ActivationFunctionType
AX_X = mybir.AxisListType.X

CONST = {}
_at = 0
for _name, _n in (("ident", P), ("later_ones", 2 * P), ("ones", P), ("mask", P), ("diff", T + 3 * P),
                  ("freq_a", 1), ("freq_r", 1)):
    CONST[_name] = (_at, _n)
    _at += _n
NCONST = _at

PARAM = {}
_at = 0
for _name, _n in (("c", 8), ("ada_b", 48), ("norm1_g", 8), ("conv_w", 32), ("conv_b", 8), ("rg_ba", 8),
                  ("rg_bx", 8), ("rg_lambda", 8), ("decay_fwd", 4), ("decay_bwd", 4), ("q_norm_g", 1),
                  ("k_norm_g", 1), ("norm2_g", 8), ("ffn_conv_w", 144), ("ffn_conv_b", 48),
                  ("a_norm_g", 8), ("a_q_norm_g", 3), ("a_kv_norm_g", 1), ("a_pool_scale", 8),
                  ("r_norm_g", 8), ("r_gn_g", 16), ("final_norm_g", 8)):
    PARAM[_name] = (_at, _n)
    _at += _n
NPARAM = _at


def ring_plan():
    units = []
    for h in range(HEADS):
        a = ADA_FIRST + ADA_HEAD * h
        units += [("q", h, 8), ("k", h, 8), ("ada", a, 8), ("v", h, 8), ("xr", h, 8), ("ada", a + 1, 8),
                  ("yr", h, 8), ("ga", h, 8), ("ada", a + 2, 8), ("gb", h, 8), ("ada", a + 3, 8)]
    units += [("w_out", m, 8) for m in range(8)]
    for t in range(THIRDS):
        for c in range(8 * t, 8 * t + 8):
            units += [("ff_g", c, 8), ("ff_v", c, 8)]
        units += [("ff_down", 8 * t + m, 8) for m in range(8)]
    units += [("kr", 0, 8), ("kr", 1, 8)] + [("cq", j, 8) for j in range(3)] + [("ckv", 0, 8)]
    for g in range(5):
        if g < 4:
            units += [("u", 2 * g, 8), ("u", 2 * g + 1, 8)]
        for c in (2 * g, 2 * g + 1):
            if g > 0:
                units += [("pool", c - 2, 2)]
            if g < 4:
                units += [("pgate", c, 8)]
    units += [("p_out", m, 8) for m in range(8)]
    units += [("qr", j, 3) for j in range(8)]
    for h in range(HEADS):
        units += [("qn", h, 3), ("kn", h, 1), ("agate", h, 8), ("vn", h, 1)]
    units += [("a_out", m, 8) for m in range(8)]
    for h in range(RH):
        units += [("rq", 2 * h, 8), ("rq", 2 * h + 1, 8), ("rk", 2 * h, 8), ("rk", 2 * h + 1, 8)]
        units += [("rv", 4 * h + c, 8) for c in range(4)] + [("rgate", 4 * h + c, 8) for c in range(4)]
        if h % 2:
            units += [("r_out", 8 * (h // 2) + m, 8) for m in range(8)]
    return units


NADA = 48
ADA_FIRST = 16
ADA_HEAD = 4
RING = ring_plan()
UNITS = [r for r in RING if r[0] != "ada"]
NU = len(UNITS)
UNIT = {(kind, j): n for n, (kind, j, _) in enumerate(UNITS)}
NA = 3
OUT_UNITS = (("w_out", 0), ("ff_down", 16), ("a_out", 0), ("r_out", 8))


def build(nc, ada, weights, params, consts, rg_w, x_t, positions, inv_counts, out_t):
    ctx = ExitStack()
    with ctx:
        def sb(name, shape, dt=F32):
            return ctx.enter_context(nc.sbuf_tensor(name, shape, dt))

        def ps(name, shape):
            return ctx.enter_context(nc.psum_tensor(name, shape, F32))

        def sem(name):
            return ctx.enter_context(nc.semaphore(name))

        par_loaded = sem("par_loaded")
        x_loaded = sem("x_loaded")
        x2_loaded = sem("x2_loaded")
        cst_loaded = sem("cst_loaded")
        rgw_loaded = sem("rgw_loaded")
        pos_loaded = sem("pos_loaded")
        inv_loaded = sem("inv_loaded")
        ada_loaded = [sem(f"ada_loaded{i}") for i in range(6)]
        raw_loaded = [sem(f"raw_loaded{i}") for i in range(NR)]
        ada_slot = [sem(f"ada_slot{i}") for i in range(NA)]
        act_order = sem("act_order")
        dve_order = sem("dve_order")
        w_high = sem("w_high")
        w_split = sem("w_split")
        unit_done = sem("unit_done")
        consts_set = sem("consts_set")
        abs_ready = sem("abs_ready")
        exp_ready = sem("exp_ready")
        ada_used = sem("ada_used")
        acc_ready = sem("acc_ready")
        mod_done = sem("mod_done")
        squared = sem("squared")
        square_used = sem("square_used")
        x_squared = sem("x_squared")
        x_summed = sem("x_summed")
        norm_summed = sem("norm_summed")
        norm_rooted = sem("norm_rooted")
        pre_h = sem("pre_h")
        h_high = sem("h_high")
        h_even = sem("h_even")
        h_odd = sem("h_odd")
        q_copied = sem("q_copied")
        k_copied = sem("k_copied")
        v_copied = sem("v_copied")
        gelu_done = sem("gelu_done")
        ga_done = sem("ga_done")
        gb_done = sem("gb_done")
        conv_started = sem("conv_started")
        conv_done = sem("conv_done")
        gate_r_done = sem("gate_r_done")
        gate_r_read = sem("gate_r_read")
        gates_done = sem("gates_done")
        gates_read = sem("gates_read")
        tanh_done = sem("tanh_done")
        decay_done = sem("decay_done")
        root_done = sem("root_done")
        y_mixed = sem("y_mixed")
        mixed = sem("mixed")
        rooted = sem("rooted")
        kq_normed = sem("kq_normed")
        vt_done = sem("vt_done")
        vt_copied = sem("vt_copied")
        z_done = sem("z_done")
        ln_done = sem("ln_done")
        lm_done = sem("lm_done")
        suffix_done = sem("suffix_done")
        att_t = sem("att_t")
        att_exp = sem("att_exp")
        att_done = sem("att_done")
        av_done = sem("av_done")
        res1_done = sem("res1_done")
        resf_done = sem("resf_done")
        resp_done = sem("resp_done")
        resa_done = sem("resa_done")
        resr_done = sem("resr_done")
        convg_started = sem("convg_started")
        convv_started = sem("convv_started")
        convg_done = sem("convg_done")
        convv_done = sem("convv_done")
        ffgelu_done = sem("ffgelu_done")
        ff_ready = sem("ff_ready")
        angle_ready = sem("angle_ready")
        sin_ready = sem("sin_ready")
        kr_read = sem("kr_read")
        qr_read = sem("qr_read")
        ropes_done = sem("ropes_done")
        rope_done = sem("rope_done")
        cq_copied = sem("cq_copied")
        ckv_copied = sem("ckv_copied")
        pre_c = sem("pre_c")
        c_high = sem("c_high")
        cqn_ready = sem("cqn_ready")
        pad_set = sem("pad_set")
        u_copied = sem("u_copied")
        d_ready = sem("d_ready")
        pgate_done = sem("pgate_done")
        pool_done = sem("pool_done")
        yp_high = sem("yp_high")
        yp_ready = sem("yp_ready")
        vn_copied = sem("vn_copied")
        qn_copied = sem("qn_copied")
        kn_copied = sem("kn_copied")
        vta_done = sem("vta_done")
        vta_copied = sem("vta_copied")
        s_done = sem("s_done")
        max_done = sem("max_done")
        p_exp = sem("p_exp")
        p_ready = sem("p_ready")
        pt_done = sem("pt_done")
        pt_copied = sem("pt_copied")
        agate_done = sem("agate_done")
        pv_done = sem("pv_done")
        ya_ready = sem("ya_ready")
        dlog_done = sem("dlog_done")
        dexp_done = sem("dexp_done")
        rq_copied = sem("rq_copied")
        rk_copied = sem("rk_copied")
        rv_copied = sem("rv_copied")
        rvt_done = sem("rvt_done")
        rvt_copied = sem("rvt_copied")
        rs_scores = sem("rs_scores")
        rs_done = sem("rs_done")
        ro_done = sem("ro_done")
        var_done = sem("var_done")
        vroot_done = sem("vroot_done")
        nmu_done = sem("nmu_done")
        on_done = sem("on_done")
        rgate_done = sem("rgate_done")
        ont_done = sem("ont_done")
        yrp_done = sem("yrp_done")
        yr_high = sem("yr_high")
        yr_ready = sem("yr_ready")
        out_ready = sem("out_ready")
        stored = sem("stored")

        raised = {}

        def counted(signal):
            raised[signal.name] = raised.get(signal.name, 0) + 1
            return raised[signal.name]

        cst = sb("cst", [P, NCONST])
        par = sb("par", [P, NPARAM])
        small = sb("small", [P, 192])
        x = sb("x", [P, DK, T])
        h_hi = sb("h_hi", [P, DK, T], F32R)
        h_lo = sb("h_lo", [P, DK, T], F32R)
        y_hi = sb("y_hi", [P, DK, T], F32R)
        y_lo = sb("y_lo", [P, DK, T], F32R)
        raw = sb("raw", [P, NR, 8 * P])
        ada_ring = sb("ada_ring", [P, NA, 2, T])
        w_hi = sb("w_hi", [P, NR, 8 * P], F32R)
        w_lo = sb("w_lo", [P, NR, 8 * P], F32R)
        scr = sb("scr", [P, 20, T])
        rgw = sb("rgw", [P, 16, P])

        lin = ps("lin", [P, 2, T])
        big = ps("big", [P, 3, T])
        m_a = ps("m_a", [P, T])
        m_b = ps("m_b", [P, T])
        m_o = ps("m_o", [P, T])
        big_f = big[:].rearrange("p a t -> p (a t)")
        ont_bank = [m_a[:], m_b[:], big[:, 0], big[:, 1]]
        ro_bank = [m_o[:], big[:, 0], big[:, 1], big[:, 2]]

        def c_(name):
            a, n = CONST[name]
            return cst[:, a:a + n]

        def p_(name, j=0):
            a, n = PARAM[name]
            return par[:, a + j:a + j + 1]

        def pall(name):
            a, n = PARAM[name]
            return par[:, a:a + n]

        def A(j, h=0):
            return scr[:, j + h % 2]

        S1 = dict(q=0, k=2, xr=4, gy=6, ya=8)
        V1, SGA, SGB = scr[:, 10], scr[:, 11], scr[:, 12]
        att_a = scr[:, 14:17].rearrange("p a t -> p (a t)")[:, 0:1280]
        att_b = scr[:, 14:19].rearrange("p a t -> p (a t)")[:, 1280:2560]
        COL = (0, 512, 1024, 896)
        KW = (512, 384, 256, 128)
        vtok = sb("vtok", [P, 2, TB, P])
        tmp = sb("tmp", [P, 4, T])
        sq_sum = sb("sq_sum", [P, T])
        sq_act = sb("sq_act", [P, 2, T])
        rstd = sb("rstd", [P, T])
        rope = rgw[:].rearrange("p a b -> p (a b)").rearrange("p (a t) -> p a t", t=T)
        posf = tmp[:, 3]
        ksr = tmp[:, 2:4]
        dtab = tmp[:, 0:2].rearrange("p a t -> p (a t)")[:, 0:T + 3 * P]

        def sm(a, n=1):
            return small[:, a:a + n]
        MOD, NEGSP, LOGG, A1, A2, GQ, C4, DC = 0, 48, 56, 64, 72, 80, 81, 90
        STAT = 130

        cq_hi = sb("cq_hi", [P, 4, T], F32R)
        cq_lo = sb("cq_lo", [P, 4, T], F32R)
        cq_sb = scr[:, 0:4]
        krr = scr[:, 4]
        qrr = scr[:, 6:10]
        sg_a = scr[:, 0:2]
        sg_p = scr[:, 6:8]
        v_fm = scr[:, 2]
        qn_sb = scr[:, 3]
        kn_sb = scr[:, 10]
        p_sb = scr[:, 11:15]
        p_t = scr[:, 15:19]
        u_pad = scr[:, 10:13].rearrange("p a t -> p (a t)")[:, 0:2 * (T + 16)].rearrange("p (a t) -> p a t", a=2)
        win = scr[:, 13:16].rearrange("p a t -> p (a t)")[:, 0:2 * (T + 16)].rearrange("p (a t) -> p a t", a=2)
        inv_count = scr[:, 16:20]
        rq_r = scr[:, 0:2]
        rk_r = scr[:, 2:4]
        s_sb = scr[:, 4:8]
        rv_fm = s_sb[:, 0:2]
        v_tk = scr[:, 8:12]
        on_sb = scr[:, 12:16]
        sg_r = scr[:, 16:20]

        eps = sb("eps", [P, 1])
        pos_i = scr[:, 19].bitcast(I32)

        ada_in = scr[:, 0:12].rearrange("p (s a) t -> p s a t", a=2)
        acc_even, acc_first = scr[:, 13:20:6], scr[:, 14:16]
        sel_r = sb("sel_r", [P, 2, P], F32R)
        lm_hi = cq_hi[:].rearrange("p a t -> p (a t)")[:, 0:1280]
        lm_lo = cq_lo[:].rearrange("p a t -> p (a t)")[:, 0:1280]
        block = ctx.enter_context(nc.Block())

        def psum_of(n):
            return lin[:, n % 2, :]

        FREED = {"q": q_copied, "k": k_copied, "v": v_copied,
                 "xr": conv_done, "yr": gelu_done, "ga": ga_done, "gb": gb_done,
                 "w_out": res1_done, "ff_down": resf_done,
                 "ff_g": convg_done, "ff_v": convv_done,
                 "cq": cq_copied, "ckv": ckv_copied, "kr": kr_read,
                 "u": u_copied, "pgate": pgate_done, "pool": pool_done,
                 "p_out": resp_done, "qr": qr_read,
                 "qn": qn_copied, "kn": kn_copied, "vn": vn_copied,
                 "agate": agate_done, "a_out": resa_done,
                 "rq": rq_copied, "rk": rk_copied, "rv": rv_copied,
                 "rgate": rgate_done, "r_out": resr_done}

        def freed(n):
            kind, j, _ = UNITS[n]
            return FREED[kind], j + 1

        @block.sync
        def _(sp):
            sp.dma_start(par[:], params).then_inc(par_loaded, 16)
            sp.dma_start(x[:, 0:4], x_t[:, 0:4]).then_inc(x_loaded, 16)
            sp.dma_start(x[:, 4:8], x_t[:, 4:8]).then_inc(x2_loaded, 16)
            sp.dma_start(cst[:], consts).then_inc(cst_loaded, 16)
            for i in range(ADA_FIRST):
                if i >= 6:
                    sp.wait_ge(ada_used, i - 5)
                sp.dma_start(ada_in[:, i % 6], ada[:, i]).then_inc(ada_loaded[i % 6], 16)
            for g, (kind, j, nk) in enumerate(RING):
                if (kind, j) == ("xr", 0):
                    sp.dma_start(rgw[:], rg_w).then_inc(rgw_loaded, 16)
                if (kind, j) == ("w_out", 7):
                    sp.wait_ge(mixed, HEADS)
                    sp.wait_ge(mod_done, 6)
                    sp.dma_start(pos_i, positions).then_inc(pos_loaded, 16)
                if (kind, j) == ("ff_g", 18):
                    sp.wait_ge(sin_ready, 4)
                    sp.dma_start(inv_count, inv_counts).then_inc(inv_loaded, 16)
                if kind == "ada":
                    r = j - ADA_FIRST
                    sp.wait_ge(ada_used, max(j - NA + 1, ADA_FIRST))
                    sp.dma_start(ada_ring[:, r % NA], ada[:, j]).then_inc(ada_slot[r % NA], 16)
                    continue
                n = UNIT[(kind, j)]
                if n >= NR:
                    sp.wait_ge(w_split, n - NR + 1)
                sp.dma_start(raw[:, n % NR, 0:nk * P], weights[n, :, 0:nk * P])\
                    .then_inc(raw_loaded[n % NR], 16)
            for k in range(DK):
                sp.wait_ge(out_ready, k + 1)
                sp.dma_start(out_t[:, k], scr[:, k]).then_inc(stored, 16)
            sp.wait_ge(stored, 16 * DK)

        @block.gpsimd
        def _(pool):
            count = [0]

            def add_square(r, m):
                pool.wait_ge(x_squared, DK * r + m + 1)
                if 6 * r + m > 1:
                    pool.wait_ge(x_summed, 6 * r + m - 1)
                nc.gpsimd.tensor_tensor(sq_sum[:], sq_sum[:], sq_act[:, m % 2], ALU.add).then_inc(x_summed, 1)

            for n in range(NU):
                s = n % NR
                for r, f in enumerate(OUT_UNITS):
                    if n == UNIT[f] + 6 + NR:
                        add_square(r, 6)
                w = UNITS[n][2] * P
                pool.wait_ge(w_high, n + 1)
                nc.gpsimd.tensor_tensor(w_lo[:, s, 0:w], raw[:, s, 0:w], w_hi[:, s, 0:w].bitcast(F32),
                                        ALU.subtract).then_inc(w_split, 1)
                for r, f in enumerate(OUT_UNITS):
                    if UNIT[f] + 1 + NR <= n < UNIT[f] + 6 + NR:
                        add_square(r, n - NR - UNIT[f])
                if n in [UNIT[f] + NR - 1 for f in (("q", 0), ("ff_g", 0), ("kr", 0), ("rq", 0))]:
                    for k in range(1, DK, 2):
                        pool.wait_ge(h_high, DK * (count[0] // 4) + k + 1)
                        nc.gpsimd.tensor_tensor(h_lo[:, k], tmp[:, k % 4], h_hi[:, k].bitcast(F32),
                                                ALU.subtract).then_inc(h_odd, 1)
                        count[0] += 1
            for m in range(5, 7):
                add_square(3, m)

        @block.tensor
        def _(pe):
            def unit(kind, j, hi, lo, ready=None, part=None):
                n = UNIT[(kind, j)]
                nk = UNITS[n][2]
                s = n % NR
                if part is None or part[0] == 0:
                    pe.wait_ge(w_split, n + 1)
                    if n >= 2:
                        f, v = freed(n - 2)
                        pe.wait_ge(f, v)
                for k in part or range(nk):
                    if ready:
                        pe.wait_ge(*ready(k))
                    wh, wl = w_hi[:, s, k * P:(k + 1) * P], w_lo[:, s, k * P:(k + 1) * P]
                    nc.tensor.matmul(psum_of(n), wh, hi(k), start=(k == 0), stop=False)
                    nc.tensor.matmul(psum_of(n), wh, lo(k), start=False, stop=False)
                    last = nc.tensor.matmul(psum_of(n), wl, hi(k), start=False, stop=(k == nk - 1))
                if k == nk - 1:
                    last.then_inc(unit_done, 1)

            def H(k):
                return h_hi[:, k]

            def L(k):
                return h_lo[:, k]

            def YH(k):
                return y_hi[:, k]

            def YL(k):
                return y_lo[:, k]

            def square(count, first, last):
                pe.wait_ge(squared, count)
                nc.tensor.matmul(m_a[:], c_("ones"), sq_act[:, count % 2], start=first, stop=last)\
                    .then_inc(square_used, 1)

            def norm_sum(r):
                pe.wait_ge(x_summed, 6 * (r + 1))
                nc.tensor.matmul(m_a[:], c_("ones"), sq_sum[:], start=True, stop=False)
                pe.wait_ge(x_squared, DK * (r + 1))
                nc.tensor.matmul(m_a[:], c_("ones"), sq_act[:, 1], start=False, stop=True)\
                    .then_inc(norm_summed, 1)

            def modulation(g):
                pe.wait_ge(acc_ready, g + 1)
                acc = acc_first if g == 1 else acc_even
                for m in range(DK):
                    out = m_o[:, 8 * g + m:8 * g + m + 1] if g < 2 else m_b[:, 8 * g - 16 + m:8 * g - 15 + m]
                    last = nc.tensor.matmul(out, acc[:, m // 4, (m % 4) * P:(m % 4 + 1) * P], c_("ones")[:, 0:1],
                                            start=True, stop=True)
                last.then_inc(mod_done, 1)

            def normed(r):
                def ready(k):
                    return (h_odd, 4 * r + k // 2 + 1) if k % 2 else (h_even, 4 * r + k // 2 + 1)
                return ready

            pe.wait_ge(cst_loaded, 16)
            pe.wait_ge(par_loaded, 16)
            for k in range(DK):
                square(k + 1, k == 0, k == DK - 1)
            modulation(0)
            modulation(1)

            for h in range(HEADS + 1):
                g = h - 1
                if h < HEADS:
                    unit("q", h, H, L, ready=None if h else normed(0))
                if g >= 0:
                    pe.wait_ge(kq_normed, 2 * g + 2)
                    pe.wait_ge(gates_read, g + 1)
                    for j in range(TB):
                        last = nc.tensor.matmul(big_f[:, COL[j]:COL[j] + KW[j]],
                                                A(S1["k"], g)[:, j * P:(j + 1) * P], A(S1["q"], g)[:, j * P:T],
                                                start=True, stop=True)
                    last.then_inc(z_done, 1)
                if h == HEADS:
                    unit("w_out", 0, YH, YL, ready=lambda k: (mixed, k + 1), part=range(7))
                if h < HEADS:
                    unit("k", h, H, L)
                    unit("v", h, H, L)
                if h == HEADS:
                    unit("w_out", 1, YH, YL, part=range(7))
                if h < HEADS:
                    if h > 0:
                        pe.wait_ge(gate_r_read, h)
                    square(8 + 2 * h + 1, True, True)
                    unit("xr", h, H, L)
                if g >= 0:
                    if h % 2 == 0:
                        modulation(1 + h // 2)
                    pe.wait_ge(lm_done, g + 1)
                    for j in range(TB):
                        for i in range(j, TB):
                            o = COL[j] + (i - j) * P
                            sel = sel_r[:, 0 if i == j else 1]
                            nc.tensor.matmul(big_f[:, o:o + KW[i]], sel, lm_hi[:, COL[i]:COL[i] + KW[i]],
                                             start=(i == j), stop=False)
                            last = nc.tensor.matmul(big_f[:, o:o + KW[i]], sel, lm_lo[:, COL[i]:COL[i] + KW[i]],
                                                    start=False, stop=(i == TB - 1))
                    last.then_inc(suffix_done, 1)
                if h < HEADS:
                    pe.wait_ge(rooted, 2 * h + 1)
                    square(8 + 2 * h + 2, True, True)
                    unit("yr", h, H, L)
                    pe.wait_ge(v_copied, h + 1)
                    if h - 1 > 0:
                        pe.wait_ge(mixed, h - 1)
                    for j in range(TB):
                        last = nc.tensor.transpose(m_o[:, j * P:(j + 1) * P], V1[:, j * P:(j + 1) * P],
                                                   c_("ident"))
                    last.then_inc(vt_done, 1)
                    unit("ga", h, H, L)
                    pe.wait_ge(vt_copied, h + 1)
                if h < HEADS:
                    unit("gb", h, H, L)
                    pe.wait_ge(rgw_loaded, 16)
                    pe.wait_ge(conv_done, h + 1)
                    pe.wait_ge(rooted, 2 * h + 2)
                    nc.tensor.matmul(m_a[:], rgw[:, h], A(S1["xr"], h), start=True, stop=True)\
                        .then_inc(gate_r_done, 1)
                    if g + 1 > 0:
                        pe.wait_ge(att_t, g + 1)
                    nc.tensor.matmul(big[:, 2], rgw[:, 8 + h], A(S1["xr"], h), start=True, stop=True)\
                        .then_inc(gates_done, 1)
                if g >= 0:
                    pe.wait_ge(att_done, g + 1)
                    for j in range(TB):
                        last = nc.tensor.matmul(m_o[:, j * P:T], vtok[:, g % 2, j],
                                                att_a[:, COL[j]:COL[j] + KW[j]],
                                                start=(j == 0), stop=(j == TB - 1))
                    last.then_inc(av_done, 1)
            pe.wait_ge(gates_read, HEADS)
            for m in range(8):
                unit("w_out", m, YH, YL, ready=None if m else lambda k: (mixed, k + 1),
                     part=range(7, DK) if m < 2 else None)
            norm_sum(0)
            for t in range(THIRDS):
                for c in range(8 * t, 8 * t + 8):
                    unit("ff_g", c, H, L, ready=None if c else normed(1))
                    unit("ff_v", c, H, L)
                for m in range(8):
                    unit("ff_down", 8 * t + m, YH, YL, ready=None if m else lambda k: (ff_ready, 8 * t + k + 1))
            norm_sum(1)
            unit("kr", 0, H, L, ready=normed(2))
            unit("kr", 1, H, L)
            for j in range(3):
                unit("cq", j, H, L)
            unit("ckv", 0, H, L)
            for g in range(5):
                if g < 4:
                    unit("u", 2 * g, H, L)
                    unit("u", 2 * g + 1, H, L)
                if g == 0:
                    pe.wait_ge(norm_rooted, 3)
                    square(25, True, False)
                    square(26, False, False)
                    square(27, False, True)

                def dh(k):
                    return y_hi[:, 2 * g - 2 + k]

                def dl(k):
                    return y_lo[:, 2 * g - 2 + k]
                if 2 * g > 0:
                    pe.wait_ge(d_ready, 2 * g)
                for c in (2 * g, 2 * g + 1):
                    if g > 0:
                        unit("pool", c - 2, dh, dl)
                    if g < 4:
                        unit("pgate", c, H, L)
                if g == 0:
                    pe.wait_ge(norm_rooted, 4)
                    square(28, True, True)
            for m in (0, 1):
                unit("p_out", m, YH, YL, part=range(6), ready=None if m else lambda k: (yp_ready, k + 1))
            for m in (0, 1):
                unit("p_out", m, YH, YL, part=range(6, 8), ready=lambda k: (yp_ready, k + 1))
            for m in range(2, 8):
                unit("p_out", m, YH, YL)
            pe.wait_ge(cqn_ready, 4)
            for j in range(8):
                unit("qr", j, lambda k: cq_hi[:, k], lambda k: cq_lo[:, k])
            for h in range(HEADS + 1):
                g = h - 1
                if h < HEADS:
                    unit("qn", h, lambda k: cq_hi[:, k], lambda k: cq_lo[:, k])
                    unit("kn", h, lambda k: cq_hi[:, 3], lambda k: cq_lo[:, 3])
                    unit("agate", h, H, L)
                    unit("vn", h, lambda k: cq_hi[:, 3], lambda k: cq_lo[:, 3])
                else:
                    for m in (0, 1):
                        unit("a_out", m, YH, YL, part=range(7), ready=None if m else lambda k: (ya_ready, k + 1))
                for transposes, b in ((True, 0), (True, 1), (False, 0), (False, 1), (True, 2), (False, 2), (True, 3),
                                      (False, 3)):
                    if g >= 0 and transposes:
                        q = 4 * g + b
                        if q - 1 > 0:
                            pe.wait_ge(pt_copied, q - 1)
                        pe.wait_ge(vta_copied, g + 1)
                        pe.wait_ge(p_ready, q + 1)
                        bank = (m_a, m_b)[q % 2]
                        for j in range(TB):
                            last = nc.tensor.transpose(bank[:, j * P:(j + 1) * P],
                                                       p_sb[:, b, j * P:(j + 1) * P], c_("ident"))
                        last.then_inc(pt_done, 1)
                    if h < HEADS and not transposes:
                        q = 4 * h + b
                        pe.wait_ge(ropes_done, 5)
                        pe.wait_ge(kn_copied, h + 1)
                        rows = slice(64 * (h % 2), 64 * (h % 2) + 64)
                        if q - 2 > 0:
                            pe.wait_ge(p_exp, q - 2)
                        cols = slice(b * P, (b + 1) * P)
                        nc.tensor.matmul(big[:, q % 3], qn_sb[:, cols], kn_sb[:], start=True, stop=False)
                        nc.tensor.matmul(big[:, q % 3], qrr[rows, h // 2, cols], krr[rows], start=False, stop=True,
                                         tile_position=(64 * (h % 2), 0)).then_inc(s_done, 1)
                if h < HEADS:
                    pe.wait_ge(vn_copied, h + 1)
                    if 4 * g + 3 > 0:
                        pe.wait_ge(pt_copied, 4 * g + 3)
                    for j in range(TB):
                        last = nc.tensor.transpose(m_a[:, j * P:(j + 1) * P], v_fm[:, j * P:(j + 1) * P],
                                                   c_("ident"))
                    last.then_inc(vta_done, 1)
                if g >= 0:
                    pe.wait_ge(pt_copied, 4 * g + 4)
                    if g > 0:
                        pe.wait_ge(ya_ready, g)
                    for j in range(TB):
                        last = nc.tensor.matmul(m_o[:], vtok[:, g % 2, j], p_t[:, j], start=(j == 0),
                                                stop=(j == TB - 1))
                    last.then_inc(pv_done, 1)
            for m in range(8):
                unit("a_out", m, YH, YL, ready=None if m else lambda k: (ya_ready, k + 1),
                     part=range(7, DK) if m < 2 else None)
            norm_sum(2)
            for h in range(RH):
                for j in range(2):
                    unit("rq", 2 * h + j, H, L, ready=None if h or j else normed(3))
                for j in range(2):
                    unit("rk", 2 * h + j, H, L)
                for c in range(5):
                    if c < 4:
                        unit("rv", 4 * h + c, H, L)
                    else:
                        unit("rgate", 4 * h, H, L)
                    if c > 0:
                        r = 4 * h + c - 1
                        pe.wait_ge(rv_copied, r + 1)
                        if r - 1 > 0:
                            pe.wait_ge(rvt_copied, r - 1)
                        if 4 * h > 0:
                            pe.wait_ge(yr_ready, 4 * h)
                        bank = (m_a, m_b)[r % 2]
                        for j in range(TB):
                            last = nc.tensor.transpose(bank[:, j * P:(j + 1) * P],
                                                       rv_fm[:, r % 2, j * P:(j + 1) * P], c_("ident"))
                        last.then_inc(rvt_done, 1)
                pe.wait_ge(rope_done, 2 * h + 2)
                if 4 * h > 0:
                    pe.wait_ge(on_done, 4 * h)
                if 4 * h > 0:
                    pe.wait_ge(yrp_done, 4 * h)
                for j in range(TB):
                    if 4 * h + j - 2 > 0:
                        pe.wait_ge(rs_done, 4 * h + j - 2)
                    for k in range(2):
                        last = nc.tensor.matmul(big[:, (4 * h + j) % 3], rk_r[:, k, j * P:(j + 1) * P], rq_r[:, k],
                                                start=(k == 0), stop=(k == 1))
                    last.then_inc(rs_scores, 1)
                unit("rgate", 4 * h + 1, H, L)
                pe.wait_ge(rs_done, 4 * h + 4)
                pe.wait_ge(rvt_copied, 4 * h + 4)
                for b in range(TB):
                    for j in range(TB):
                        last = nc.tensor.matmul(ro_bank[b], s_sb[:, j, b * P:(b + 1) * P], v_tk[:, j],
                                                start=(j == 0), stop=(j == TB - 1))
                    last.then_inc(ro_done, 1)
                unit("rgate", 4 * h + 2, H, L)
                unit("rgate", 4 * h + 3, H, L)
                pe.wait_ge(on_done, 4 * h + 4)
                for c in range(4):
                    for b in range(TB):
                        last = nc.tensor.transpose(ont_bank[c][:, b * P:(b + 1) * P], on_sb[:, b, c * P:(c + 1) * P],
                                                   c_("ident"))
                    last.then_inc(ont_done, 1)
                if h % 2:
                    for m in (0, 1):
                        unit("r_out", 8 * (h // 2) + m, YH, YL, part=range(4))
                    for m in (0, 1):
                        unit("r_out", 8 * (h // 2) + m, YH, YL, part=range(4, 8),
                             ready=lambda k: (yr_ready, 8 * (h // 2) + k + 1))
                    for m in range(2, 8):
                        unit("r_out", 8 * (h // 2) + m, YH, YL)
            norm_sum(3)

        @block.scalar
        def _(act):
            issued = [0]

            def split_ahead(n):
                while issued[0] < min(n + AHEAD + 1, NU):
                    u = issued[0]
                    s = u % NR
                    wd = UNITS[u][2] * P
                    act.wait_ge(raw_loaded[s], 16 * (u // NR + 1))
                    if u - NR + 1 > 0:
                        act.wait_ge(unit_done, u - NR + 1)
                    nc.scalar.activation(w_hi[:, s, 0:wd], raw[:, s, 0:wd], ACT.Copy).then_inc(w_high, 1)
                    act.wait_ge(w_high, counted(w_high))
                    issued[0] += 1

            def at(kind, j):
                n = UNIT[(kind, j)]
                split_ahead(n if (kind, j) not in (("ga", HEADS - 1), ("gb", HEADS - 1)) else UNIT[("gb", HEADS - 1)] - AHEAD)
                act.wait_ge(unit_done, n + 1)
                return psum_of(n)

            def root(total, signal):
                nc.scalar.activation(rstd[:], m_a[:], ACT.Ln, bias=eps[:, 0:1],
                                     scale=1.0 / total).then_inc(act_order, 1)
                act.wait_ge(act_order, counted(act_order))
                nc.scalar.activation(rstd[:], rstd[:], ACT.Exp, scale=-0.5).then_inc(signal, 1)
                act.wait_ge(signal, counted(signal))

            def square(count, src):
                if count - 2 > 0:
                    act.wait_ge(square_used, count - 2)
                nc.scalar.activation(sq_act[:, count % 2], src, ACT.Square).then_inc(squared, 1)
                act.wait_ge(squared, counted(squared))

            def x_square(r, m):
                if m == 1:
                    act.wait_ge(square_used, 24 if r < 2 else 28)
                    if r > 0:
                        act.wait_ge(norm_summed, r)
                if (6 * r + m - 2 if m > 2 else 0) > 0:
                    act.wait_ge(x_summed, 6 * r + m - 2 if m > 2 else 0)
                nc.scalar.activation(sq_act[:, m % 2] if m else sq_sum[:], x[:, m], ACT.Square).then_inc(x_squared, 1)
                act.wait_ge(x_squared, counted(x_squared))
                if m == DK - 2:
                    nc.scalar.activation(sm(183), eps[:, 0:1], ACT.Ln).then_inc(act_order, 1)
                    act.wait_ge(act_order, counted(act_order))

            def norm_root(summed, count, total):
                act.wait_ge(summed, count)
                root(total, norm_rooted)

            def highs(r):
                for k in range(DK):
                    act.wait_ge(pre_h, DK * r + k + 1)
                    nc.scalar.activation(h_hi[:, k], tmp[:, k % 4], ACT.Copy).then_inc(h_high, 1)
                    act.wait_ge(h_high, counted(h_high))

            act.wait_ge(consts_set, 1)
            act.wait_ge(abs_ready, 1)
            nc.scalar.activation(sm(DC + 16, 16), sm(DC, 16), ACT.Exp, scale=-1.0).then_inc(exp_ready, 1)
            act.wait_ge(exp_ready, counted(exp_ready))
            act.wait_ge(x_loaded, 16)
            act.wait_ge(x2_loaded, 16)
            for k in range(DK):
                square(k + 1, x[:, k])
            norm_root(square_used, 8, D)
            split_ahead(0)
            highs(0)
            for h in range(HEADS + 1):
                g = h - 1
                if h == HEADS:
                    split_ahead(UNIT[("w_out", 0)])
                if h < HEADS:
                    i = at("q", h)
                    nc.scalar.activation(A(S1["q"], h), i, ACT.Copy).then_inc(q_copied, 1)
                    act.wait_ge(q_copied, counted(q_copied))
                    square(9 + 2 * h, A(S1["q"], h))
                if g >= 0:
                    act.wait_ge(z_done, g + 1)
                    nc.scalar.activation(att_a, big_f[:, 0:1280], ACT.Abs).then_inc(act_order, 1)
                    act.wait_ge(act_order, counted(act_order))
                    nc.scalar.activation(att_a, att_a, ACT.Exp, scale=-1.0).then_inc(act_order, 1)
                    act.wait_ge(act_order, counted(act_order))
                    nc.scalar.activation(att_a, att_a, ACT.Ln, bias=1.0).then_inc(ln_done, 1)
                    act.wait_ge(ln_done, counted(ln_done))
                if h < HEADS:
                    i = at("k", h)
                    nc.scalar.activation(A(S1["k"], h), i, ACT.Copy).then_inc(k_copied, 1)
                    act.wait_ge(k_copied, counted(k_copied))
                    square(10 + 2 * h, A(S1["k"], h))
                    i = at("v", h)
                    nc.scalar.activation(V1, i, ACT.Copy).then_inc(v_copied, 1)
                    act.wait_ge(v_copied, counted(v_copied))
                    act.wait_ge(square_used, 8 + 2 * h + 1)
                    if 2 * h > 0:
                        act.wait_ge(kq_normed, 2 * h)
                    root(P, rooted)
                if h < HEADS:
                    i = at("xr", h)
                    nc.scalar.activation(A(S1["xr"], h), i, ACT.Identity, bias=p_("conv_b", h),
                                         scale=p_("conv_w", 24 + h)).then_inc(conv_started, 1)
                    act.wait_ge(conv_started, counted(conv_started))
                if h < HEADS:
                    act.wait_ge(square_used, 8 + 2 * h + 2)
                    act.wait_ge(kq_normed, 2 * h + 1)
                    root(P, rooted)
                    i = at("yr", h)
                    nc.scalar.activation(A(S1["gy"], h), i, ACT.Gelu_apprx_tanh).then_inc(gelu_done, 1)
                    act.wait_ge(gelu_done, counted(gelu_done))
                if g >= 0:
                    act.wait_ge(att_t, g + 1)
                    nc.scalar.activation(att_a, att_a, ACT.Exp).then_inc(att_exp, 1)
                    act.wait_ge(att_exp, counted(att_exp))
                if h < HEADS:
                    act.wait_ge(vt_done, h + 1)
                    nc.scalar.activation(vtok[:, h % 2], m_o[:].rearrange("p (j d) -> p j d", j=TB),
                                         ACT.Copy).then_inc(vt_copied, 1)
                    act.wait_ge(vt_copied, counted(vt_copied))
                    i = at("ga", h)
                    if h > 0:
                        act.wait_ge(y_mixed, h)
                    nc.scalar.activation(SGA, i, ACT.Sigmoid).then_inc(ga_done, 1)
                    act.wait_ge(ga_done, counted(ga_done))
                    act.wait_ge(gate_r_done, h + 1)
                    nc.scalar.activation(tmp[:, 0], m_a[:], ACT.Sigmoid, bias=p_("rg_ba", h)).then_inc(gate_r_read, 1)
                    act.wait_ge(gate_r_read, counted(gate_r_read))
                    nc.scalar.activation(tmp[:, 0], tmp[:, 0], ACT.Tanh, scale=sm(C4 + h)).then_inc(tanh_done, 1)
                    act.wait_ge(tanh_done, counted(tanh_done))
                    i = at("gb", h)
                    if h > 0:
                        act.wait_ge(mixed, h)
                    nc.scalar.activation(SGB, i, ACT.Sigmoid).then_inc(gb_done, 1)
                    act.wait_ge(gb_done, counted(gb_done))
                    act.wait_ge(gates_done, h + 1)
                    nc.scalar.activation(tmp[:, 1], big[:, 2], ACT.Sigmoid, bias=p_("rg_bx",
                                         h)).then_inc(gates_read, 1)
                    act.wait_ge(gates_read, counted(gates_read))
                    act.wait_ge(decay_done, h + 1)
                    nc.scalar.activation(tmp[:, 0], tmp[:, 0], ACT.Sqrt).then_inc(root_done, 1)
                    act.wait_ge(root_done, counted(root_done))
            for m in range(8):
                split_ahead(UNIT[("w_out", m)])
                act.wait_ge(res1_done, m + 1)
                x_square(0, m)
            split_ahead(UNIT[("ff_g", 0)])
            norm_root(norm_summed, 1, D)
            highs(1)
            for t in range(THIRDS):
                for c in range(8 * t, 8 * t + 8):
                    b = c % 2
                    i = at("ff_g", c)
                    if c - 1 > 0:
                        act.wait_ge(ff_ready, c - 1)
                    nc.scalar.activation(scr[:, b], i, ACT.Identity, bias=p_("ffn_conv_b", c),
                                         scale=p_("ffn_conv_w", 96 + c)).then_inc(convg_started, 1)
                    act.wait_ge(convg_started, counted(convg_started))
                    i = at("ff_v", c)
                    nc.scalar.activation(scr[:, 2 + b], i, ACT.Identity, bias=p_("ffn_conv_b", 24 + c),
                                         scale=p_("ffn_conv_w", 120 + c)).then_inc(convv_started, 1)
                    act.wait_ge(convv_started, counted(convv_started))
                    act.wait_ge(convg_done, c + 1)
                    nc.scalar.activation(scr[:, b], scr[:, b], ACT.Gelu_apprx_tanh).then_inc(ffgelu_done, 1)
                    act.wait_ge(ffgelu_done, counted(ffgelu_done))
                    if c in (5, 8, 11, 14):
                        act.wait_ge(angle_ready, (c - 2) // 3)
                        nc.scalar.activation(rope[:, (c - 5) // 3], scr[:, 4], ACT.Sin).then_inc(sin_ready, 1)
                        act.wait_ge(sin_ready, counted(sin_ready))
                for m in range(8):
                    split_ahead(UNIT[("ff_down", 8 * t + m)])
                    act.wait_ge(resf_done, 8 * t + m + 1)
                    if t == 2:
                        x_square(1, m)
            split_ahead(UNIT[("kr", 0)])
            norm_root(norm_summed, 2, D)
            highs(2)
            for j in range(2):
                at("kr", j)
            for j in range(3):
                i = at("cq", j)
                nc.scalar.activation(cq_sb[:, j], i, ACT.Copy).then_inc(cq_copied, 1)
                act.wait_ge(cq_copied, counted(cq_copied))
                if j < 2:
                    square(25 + j, cq_sb[:, j])
            i = at("ckv", 0)
            nc.scalar.activation(cq_sb[:, 3], i, ACT.Copy).then_inc(ckv_copied, 1)
            act.wait_ge(ckv_copied, counted(ckv_copied))
            square(27, cq_sb[:, 2])
            for g in range(5):
                if g < 4:
                    for c in (2 * g, 2 * g + 1):
                        i = at("u", c)
                        act.wait_ge(pad_set, 1)
                        if 2 * g > 0:
                            act.wait_ge(d_ready, 2 * g)
                        nc.scalar.activation(u_pad[:, c % 2, 8:8 + T], i, ACT.Copy).then_inc(u_copied, 1)
                        act.wait_ge(u_copied, counted(u_copied))
                if g == 0:
                    norm_root(square_used, 27, 384)
                    square(28, cq_sb[:, 3])
                    for j in range(3):
                        act.wait_ge(pre_c, j + 1)
                        nc.scalar.activation(cq_hi[:, j], tmp[:, j], ACT.Copy).then_inc(c_high, 1)
                        act.wait_ge(c_high, counted(c_high))
                for c in (2 * g, 2 * g + 1):
                    if g > 0:
                        split_ahead(UNIT[("pool", c - 2)])
                    if g > 0 and c % 2:
                        act.wait_ge(pool_done, 2 * g)
                        for k in (2 * g - 2, 2 * g - 1):
                            nc.scalar.activation(y_hi[:, k], tmp[:, k % 2], ACT.Copy).then_inc(yp_high, 1)
                            act.wait_ge(yp_high, counted(yp_high))
                    if g < 4:
                        i = at("pgate", c)
                        if c - 1 > 0:
                            act.wait_ge(pool_done, c - 1)
                        nc.scalar.activation(sg_p[:, c % 2], i, ACT.Silu).then_inc(pgate_done, 1)
                        act.wait_ge(pgate_done, counted(pgate_done))
                if g == 0:
                    norm_root(square_used, 28, P)
                    act.wait_ge(pre_c, 4)
                    nc.scalar.activation(cq_hi[:, 3], tmp[:, 3], ACT.Copy).then_inc(c_high, 1)
                    act.wait_ge(c_high, counted(c_high))
            for m in range(8):
                split_ahead(UNIT[("p_out", m)])
                act.wait_ge(unit_done, UNIT[("p_out", m)] + 1)
            for j in range(8):
                at("qr", j)
            for h in range(HEADS + 1):
                g = h - 1
                if h < HEADS:
                    i = at("qn", h)
                    if 4 * h > 0:
                        act.wait_ge(s_done, 4 * h)
                    nc.scalar.activation(qn_sb, i, ACT.Copy).then_inc(qn_copied, 1)
                    act.wait_ge(qn_copied, counted(qn_copied))
                    i = at("kn", h)
                    nc.scalar.activation(kn_sb, i, ACT.Copy).then_inc(kn_copied, 1)
                    act.wait_ge(kn_copied, counted(kn_copied))
                    i = at("agate", h)
                    if h - 1 > 0:
                        act.wait_ge(ya_ready, h - 1)
                    nc.scalar.activation(sg_a[:, h % 2], i, ACT.Silu).then_inc(agate_done, 1)
                    act.wait_ge(agate_done, counted(agate_done))
                    i = at("vn", h)
                    if h > 0:
                        act.wait_ge(vta_done, h)
                    nc.scalar.activation(v_fm, i, ACT.Copy).then_inc(vn_copied, 1)
                    act.wait_ge(vn_copied, counted(vn_copied))
                else:
                    split_ahead(UNIT[("a_out", 0)])
                for transposes, b in ((True, 0), (True, 1), (False, 0), (True, 2), (False, 1), (True, 3), (False, 2),
                                      (False, 3)):
                    if g >= 0 and transposes:
                        act.wait_ge(pt_done, 4 * g + b + 1)
                        if g > 0:
                            act.wait_ge(pv_done, g)
                        nc.scalar.activation(p_t[:, :, b * P:(b + 1) * P], (m_a,
                                             m_b)[b % 2][:].rearrange("p (j d) -> p j d", j=TB), ACT.Copy)\
                            .then_inc(pt_copied, 1)
                        act.wait_ge(pt_copied, counted(pt_copied))
                    if h < HEADS and not transposes:
                        q = 4 * h + b
                        act.wait_ge(max_done, q + 1)
                        nc.scalar.activation(p_sb[:, b], big[:, q % 3], ACT.Exp, bias=sm(STAT + b),
                                             scale=192.0 ** -0.5, accum_out=sm(STAT + 4 + b)).then_inc(p_exp, 1)
                        act.wait_ge(p_exp, counted(p_exp))
                if h < HEADS:
                    act.wait_ge(vta_done, h + 1)
                    nc.scalar.activation(vtok[:, h % 2], m_a[:].rearrange("p (j d) -> p j d", j=TB),
                                         ACT.Copy).then_inc(vta_copied, 1)
                    act.wait_ge(vta_copied, counted(vta_copied))
            for m in range(8):
                split_ahead(UNIT[("a_out", m)])
                act.wait_ge(resa_done, m + 1)
                x_square(2, m)
            split_ahead(UNIT[("rq", 0)])
            norm_root(norm_summed, 3, D)
            highs(3)
            for h in range(RH):
                for j in range(2):
                    i = at("rq", 2 * h + j)
                    nc.scalar.activation(rq_r[:, j], i, ACT.Copy).then_inc(rq_copied, 1)
                    act.wait_ge(rq_copied, counted(rq_copied))
                for j in range(2):
                    i = at("rk", 2 * h + j)
                    nc.scalar.activation(rk_r[:, j], i, ACT.Copy).then_inc(rk_copied, 1)
                    act.wait_ge(rk_copied, counted(rk_copied))
                act.wait_ge(dlog_done, h + 1)
                nc.scalar.activation(dtab, dtab, ACT.Exp).then_inc(dexp_done, 1)
                act.wait_ge(dexp_done, counted(dexp_done))
                for c in range(5):
                    if c < 4:
                        i = at("rv", 4 * h + c)
                        nc.scalar.activation(rv_fm[:, c % 2], i, ACT.Copy).then_inc(rv_copied, 1)
                        act.wait_ge(rv_copied, counted(rv_copied))
                    else:
                        i = at("rgate", 4 * h)
                        nc.scalar.activation(sg_r[:, 0], i, ACT.Silu).then_inc(rgate_done, 1)
                        act.wait_ge(rgate_done, counted(rgate_done))
                    if c > 0:
                        r = 4 * h + c - 1
                        act.wait_ge(rvt_done, r + 1)
                        nc.scalar.activation(v_tk[:, :, (c - 1) * P:c * P], (m_a,
                                             m_b)[r % 2][:].rearrange("p (j d) -> p j d", j=TB), ACT.Copy)\
                            .then_inc(rvt_copied, 1)
                        act.wait_ge(rvt_copied, counted(rvt_copied))
                i = at("rgate", 4 * h + 1)
                nc.scalar.activation(sg_r[:, 1], i, ACT.Silu).then_inc(rgate_done, 1)
                act.wait_ge(rgate_done, counted(rgate_done))
                for b in range(TB):
                    act.wait_ge(var_done, 4 * h + b + 1)
                    nc.scalar.activation(sm(STAT + 16), sm(STAT + 9), ACT.Sqrt, bias=eps[:,
                                         0:1]).then_inc(vroot_done, 1)
                    act.wait_ge(vroot_done, counted(vroot_done))
                    act.wait_ge(nmu_done, 4 * h + b + 1)
                    nc.scalar.activation(on_sb[:, b], ro_bank[b], ACT.Identity, bias=sm(STAT + 18),
                                         scale=sm(STAT + 17)).then_inc(on_done, 1)
                    act.wait_ge(on_done, counted(on_done))
                for c in (2, 3):
                    i = at("rgate", 4 * h + c)
                    nc.scalar.activation(sg_r[:, c], i, ACT.Silu).then_inc(rgate_done, 1)
                    act.wait_ge(rgate_done, counted(rgate_done))
                for c in range(4):
                    act.wait_ge(yrp_done, 4 * h + c + 1)
                    nc.scalar.activation(y_hi[:, 4 * (h % 2) + c], tmp[:, c % 2], ACT.Copy).then_inc(yr_high, 1)
                    act.wait_ge(yr_high, counted(yr_high))
                if h % 2:
                    for m in range(8):
                        r = 8 * (h // 2) + m
                        split_ahead(UNIT[("r_out", r)])
                        act.wait_ge(resr_done, r + 1)
                        if h == 3:
                            x_square(3, m)
            norm_root(norm_summed, 4, D)


        @block.vector
        def _(dve):
            v = nc.vector

            M, AD, SU, MX, MN = ALU.mult, ALU.add, ALU.subtract, ALU.max, ALU.min

            v.memset(eps[:], EPS).then_inc(consts_set, 1)
            dve.wait_ge(consts_set, counted(consts_set))

            def accumulate(a):
                g, k = divmod(a, DK)
                if a < ADA_FIRST:
                    dve.wait_ge(ada_loaded[a % 6], 16 * (a // 6 + 1))
                    src = ada_in[:, a % 6]
                else:
                    r = a - ADA_FIRST
                    dve.wait_ge(ada_slot[r % NA], 16 * (r // NA + 1))
                    src = ada_ring[:, r % NA]
                    if (g if k == 0 else 0) > 0:
                        dve.wait_ge(mod_done, g if k == 0 else 0)
                acc = acc_first if g == 1 else acc_even
                if k == 0:
                    v.tensor_scalar(acc, src, p_("c", k), None, M).then_inc(ada_used, 1)
                    dve.wait_ge(ada_used, counted(ada_used))
                else:
                    v.scalar_tensor_tensor(out=acc, in0=src, scalar=p_("c", k), in1=acc, op0=M,
                                           op1=AD).then_inc(ada_used, 1)
                    dve.wait_ge(ada_used, counted(ada_used))
                if k == DK - 1:
                    v.tensor_scalar(sm(STAT + 19), eps[:, 0:1], 1.0, None, M).then_inc(acc_ready, 1)
                    dve.wait_ge(acc_ready, counted(acc_ready))
            dve.wait_ge(par_loaded, 16)
            d0 = PARAM["rg_lambda"][0]
            d16 = par[:, d0:d0 + 16]
            v.scalar_tensor_tensor(out=sm(DC, 16), in0=d16, scalar=-1.0, in1=d16, op0=M,
                                   op1=MX).then_inc(abs_ready, 1)
            dve.wait_ge(abs_ready, counted(abs_ready))
            dve.wait_ge(cst_loaded, 16)
            v.tensor_copy(sel_r[:].rearrange("p a b -> p (a b)"), c_("later_ones")).then_inc(dve_order, 1)
            dve.wait_ge(dve_order, counted(dve_order))
            def norm_apply(r, gain, shift=None):
                dve.wait_ge(norm_rooted, {0: 1, 1: 2, 2: 3, 3: 6}[r])
                for k in range(DK + 1):
                    if k < DK:
                        if (4 * r + (k - 4) // 2 + 1 if k >= 4 and k % 2 else 0) > 0:
                            dve.wait_ge(h_odd, 4 * r + (k - 4) // 2 + 1 if k >= 4 and k % 2 else 0)
                        if shift is None:
                            v.scalar_tensor_tensor(out=tmp[:, k % 4], in0=x[:, k], scalar=gain(k), in1=rstd[:],
                                                   op0=M, op1=M).then_inc(pre_h, 1)
                            dve.wait_ge(pre_h, counted(pre_h))
                        else:
                            v.scalar_tensor_tensor(out=tmp[:, k % 4], in0=x[:, k], scalar=gain(k), in1=rstd[:],
                                                   op0=M, op1=M).then_inc(dve_order, 1)
                            dve.wait_ge(dve_order, counted(dve_order))
                            v.tensor_scalar(tmp[:, k % 4], tmp[:, k % 4], shift(k), None, AD).then_inc(pre_h, 1)
                            dve.wait_ge(pre_h, counted(pre_h))
                    if k % 2:
                        e = k - 1
                        dve.wait_ge(h_high, DK * r + e + 1)
                        v.tensor_tensor(h_lo[:, e], tmp[:, e % 4], h_hi[:, e].bitcast(F32), SU).then_inc(h_even, 1)
                        dve.wait_ge(h_even, counted(h_even))
                dve.wait_ge(h_odd, 4 * r + 4)

            for a in range(ADA_FIRST):
                accumulate(a)
            dve.wait_ge(mod_done, 2)
            a0 = PARAM["ada_b"][0]
            v.tensor_tensor(sm(MOD, 16), m_o[:, 0:16], par[:, a0:a0 + 16], AD).then_inc(dve_order, 1)
            dve.wait_ge(dve_order, counted(dve_order))
            v.scalar_tensor_tensor(out=sm(A1, 8), in0=sm(MOD + 8, 8), scalar=1.0, in1=pall("norm1_g"), op0=AD,
                                   op1=M).then_inc(dve_order, 1)
            dve.wait_ge(dve_order, counted(dve_order))
            dve.wait_ge(x_loaded, 16)
            dve.wait_ge(x2_loaded, 16)
            norm_apply(0, lambda k: sm(A1 + k), shift=lambda k: sm(MOD + k))
            dve.wait_ge(exp_ready, 1)
            e = sm(DC + 16, 16)
            r = sm(DC + 32, 8)
            t_ = small[:, DC:DC + 16]
            s_ = small[:, 150:166]
            s2 = small[:, 166:182]
            v.tensor_scalar(t_, e, 2.0, None, AD).then_inc(dve_order, 1)
            dve.wait_ge(dve_order, counted(dve_order))
            v.reciprocal(t_, t_).then_inc(dve_order, 1)
            dve.wait_ge(dve_order, counted(dve_order))
            v.tensor_tensor(s_, e, t_, M).then_inc(dve_order, 1)
            dve.wait_ge(dve_order, counted(dve_order))
            v.tensor_tensor(s2, s_, s_, M).then_inc(dve_order, 1)
            dve.wait_ge(dve_order, counted(dve_order))
            v.tensor_scalar(t_, s2, 1.0 / 15, 1.0 / 13, M, AD).then_inc(dve_order, 1)
            dve.wait_ge(dve_order, counted(dve_order))
            for c in (11, 9, 7, 5, 3, 1):
                v.tensor_tensor(t_, t_, s2, M).then_inc(dve_order, 1)
                dve.wait_ge(dve_order, counted(dve_order))
                v.tensor_scalar(t_, t_, 1.0 / c, None, AD).then_inc(dve_order, 1)
                dve.wait_ge(dve_order, counted(dve_order))
            v.scalar_tensor_tensor(out=s_, in0=s_, scalar=2.0, in1=t_, op0=M, op1=M).then_inc(dve_order, 1)
            dve.wait_ge(dve_order, counted(dve_order))
            v.tensor_scalar(t_, d16, -1.0, 0.0, M, MX).then_inc(dve_order, 1)
            dve.wait_ge(dve_order, counted(dve_order))
            v.tensor_tensor(s_, s_, t_, AD).then_inc(dve_order, 1)
            dve.wait_ge(dve_order, counted(dve_order))
            v.tensor_scalar(sm(C4, 8), s_[:, 0:8], RG_C / 2, None, M).then_inc(dve_order, 1)
            dve.wait_ge(dve_order, counted(dve_order))
            v.tensor_scalar(sm(LOGG, 8), s_[:, 8:16], -1.0, None, M).then_inc(dve_order, 1)
            dve.wait_ge(dve_order, counted(dve_order))
            v.tensor_scalar(sm(GQ), p_("q_norm_g"), float(P) ** -0.5, None, M).then_inc(dve_order, 1)
            dve.wait_ge(dve_order, counted(dve_order))

            z = big_f[:, 0:1280]
            for h in range(HEADS + 1):
                g = h - 1
                if g >= 0:
                    dve.wait_ge(z_done, g + 1)
                    dve.wait_ge(ln_done, g + 1)
                    v.scalar_tensor_tensor(out=att_a, in0=z, scalar=0.0, in1=att_a, op0=MN,
                                           op1=SU).then_inc(dve_order, 1)
                    dve.wait_ge(dve_order, counted(dve_order))
                    v.tensor_tensor(att_b, att_a, z, SU).then_inc(dve_order, 1)
                    dve.wait_ge(dve_order, counted(dve_order))
                    for j in range(TB):
                        o = att_b[:, COL[j]:COL[j] + P]
                        v.tensor_tensor(o, o, c_("mask"), M).then_inc(dve_order, 1)
                        dve.wait_ge(dve_order, counted(dve_order))
                    v.tensor_copy(lm_hi, att_b).then_inc(dve_order, 1)
                    dve.wait_ge(dve_order, counted(dve_order))
                    v.tensor_tensor(lm_lo, att_b, lm_hi.bitcast(F32), SU).then_inc(lm_done, 1)
                    dve.wait_ge(lm_done, counted(lm_done))
                if h < HEADS:
                    accumulate(ADA_FIRST + 4 * h)
                    dve.wait_ge(rooted, 2 * h + 1)
                    q = A(S1["q"], h)
                    v.scalar_tensor_tensor(out=q, in0=q, scalar=sm(GQ), in1=rstd[:], op0=M,
                                           op1=M).then_inc(kq_normed, 1)
                    dve.wait_ge(kq_normed, counted(kq_normed))
                    accumulate(ADA_FIRST + 4 * h + 1)
                if h < HEADS:
                    dve.wait_ge(conv_started, h + 1)
                    n = UNIT[("xr", h)]
                    xr = A(S1["xr"], h)
                    for s in (1, 2, 3):
                        signal = conv_done if s == 3 else dve_order
                        v.scalar_tensor_tensor(out=xr[:, s:T], in0=psum_of(n)[:, 0:T - s], scalar=p_("conv_w",
                                               8 * (3 - s) + h), in1=xr[:, s:T], op0=M, op1=AD).then_inc(signal, 1)
                        dve.wait_ge(signal, counted(signal))
                if g >= 0:
                    dve.wait_ge(suffix_done, g + 1)
                    v.tensor_tensor(att_a, att_a, z, AD).then_inc(att_t, 1)
                    dve.wait_ge(att_t, counted(att_t))
                if h < HEADS:
                    dve.wait_ge(rooted, 2 * h + 2)
                    k = A(S1["k"], h)
                    v.scalar_tensor_tensor(out=k, in0=k, scalar=p_("k_norm_g"), in1=rstd[:], op0=M,
                                           op1=M).then_inc(kq_normed, 1)
                    dve.wait_ge(kq_normed, counted(kq_normed))
                    accumulate(ADA_FIRST + 4 * h + 2)
                if g >= 0:
                    dve.wait_ge(att_exp, g + 1)
                    for j in range(TB):
                        o = att_a[:, COL[j]:COL[j] + P]
                        signal = att_done if j == TB - 1 else dve_order
                        v.tensor_tensor(o, o, c_("mask"), M).then_inc(signal, 1)
                        dve.wait_ge(signal, counted(signal))
                    dve.wait_ge(av_done, g + 1)
                    v.tensor_tensor(tmp[:, 3], m_o[:], SGB, M).then_inc(dve_order, 1)
                    dve.wait_ge(dve_order, counted(dve_order))
                    v.tensor_tensor(tmp[:, 3], tmp[:, 3], A(S1["ya"], g), AD).then_inc(dve_order, 1)
                    dve.wait_ge(dve_order, counted(dve_order))
                    v.tensor_copy(y_hi[:, g], tmp[:, 3]).then_inc(dve_order, 1)
                    dve.wait_ge(dve_order, counted(dve_order))
                    v.tensor_tensor(y_lo[:, g], tmp[:, 3], y_hi[:, g].bitcast(F32), SU).then_inc(mixed, 1)
                    dve.wait_ge(mixed, counted(mixed))
                if h < HEADS:
                    dve.wait_ge(tanh_done, h + 1)
                    v.tensor_scalar(tmp[:, 2], tmp[:, 0], 1.0, None, AD).then_inc(decay_done, 1)
                    dve.wait_ge(decay_done, counted(decay_done))
                    v.reciprocal(tmp[:, 2], tmp[:, 2]).then_inc(dve_order, 1)
                    dve.wait_ge(dve_order, counted(dve_order))
                    dve.wait_ge(gates_read, h + 1)
                    v.tensor_tensor(tmp[:, 1], tmp[:, 1], xr, M).then_inc(dve_order, 1)
                    dve.wait_ge(dve_order, counted(dve_order))
                    dve.wait_ge(root_done, h + 1)
                    v.scalar_tensor_tensor(out=tmp[:, 0], in0=tmp[:, 0], scalar=2.0, in1=tmp[:, 2], op0=M,
                                           op1=M).then_inc(dve_order, 1)
                    dve.wait_ge(dve_order, counted(dve_order))
                    v.tensor_tensor(tmp[:, 1], tmp[:, 1], tmp[:, 0], M).then_inc(dve_order, 1)
                    dve.wait_ge(dve_order, counted(dve_order))
                    v.tensor_scalar(tmp[:, 2], tmp[:, 2], 2.0, -1.0, M, AD).then_inc(dve_order, 1)
                    dve.wait_ge(dve_order, counted(dve_order))
                    v.tensor_tensor_scan(tmp[:, 0], tmp[:, 2], tmp[:, 1], 0.0, M, AD).then_inc(dve_order, 1)
                    dve.wait_ge(dve_order, counted(dve_order))
                    dve.wait_ge(gelu_done, h + 1)
                    v.tensor_tensor(tmp[:, 0], tmp[:, 0], A(S1["gy"], h), M).then_inc(dve_order, 1)
                    dve.wait_ge(dve_order, counted(dve_order))
                    dve.wait_ge(ga_done, h + 1)
                    v.tensor_tensor(A(S1["ya"], h), tmp[:, 0], SGA, M).then_inc(y_mixed, 1)
                    dve.wait_ge(y_mixed, counted(y_mixed))
                    accumulate(ADA_FIRST + 4 * h + 3)
            dve.wait_ge(mod_done, 6)
            v.tensor_tensor(sm(MOD + 16, 32), m_b[:, 0:32], par[:, a0 + 16:a0 + 48], AD).then_inc(dve_order, 1)
            dve.wait_ge(dve_order, counted(dve_order))
            v.scalar_tensor_tensor(out=sm(A2, 8), in0=sm(MOD + 32, 8), scalar=1.0, in1=pall("norm2_g"), op0=AD,
                                   op1=M).then_inc(dve_order, 1)
            dve.wait_ge(dve_order, counted(dve_order))
            for m in range(8):
                n = UNIT[("w_out", m)]
                dve.wait_ge(unit_done, n + 1)
                v.scalar_tensor_tensor(out=x[:, m], in0=psum_of(n), scalar=sm(MOD + 16 + m), in1=x[:, m],
                                       op0=M, op1=AD).then_inc(res1_done, 1)
                dve.wait_ge(res1_done, counted(res1_done))
            MAGIC, TWO_PI = 12582912.0, 2.0 * np.pi
            C1 = 6.28125
            C2 = float(np.floor((TWO_PI - C1) * 2.0 ** 20)) * 2.0 ** -20
            C3 = TWO_PI - C1 - C2
            PI_SAFE = float(np.nextafter(np.float32(np.pi), np.float32(0)))

            def angle(r, step):
                quarter = 0.25 * (r % 2)
                if step == 0:
                    if r == 0:
                        dve.wait_ge(pos_loaded, 16)
                        v.tensor_copy(posf, pos_i).then_inc(dve_order, 1)
                        dve.wait_ge(dve_order, counted(dve_order))
                    v.tensor_scalar(tmp[:, 1], posf, c_("freq_a") if r < 2 else c_("freq_r"), None,
                                    M).then_inc(dve_order, 1)
                    dve.wait_ge(dve_order, counted(dve_order))
                    v.tensor_scalar(tmp[:, 2], tmp[:, 1], 1.0 / TWO_PI, quarter, M, AD).then_inc(dve_order, 1)
                    dve.wait_ge(dve_order, counted(dve_order))
                    v.tensor_scalar(tmp[:, 2], tmp[:, 2], MAGIC, None, AD).then_inc(dve_order, 1)
                    dve.wait_ge(dve_order, counted(dve_order))
                if step == 1:
                    v.tensor_scalar(tmp[:, 2], tmp[:, 2], MAGIC, None, SU).then_inc(dve_order, 1)
                    dve.wait_ge(dve_order, counted(dve_order))
                    for part in (C1, C2):
                        v.scalar_tensor_tensor(out=tmp[:, 1], in0=tmp[:, 2], scalar=-part, in1=tmp[:, 1],
                                               op0=M, op1=AD).then_inc(dve_order, 1)
                        dve.wait_ge(dve_order, counted(dve_order))
                if step == 2:
                    v.scalar_tensor_tensor(out=tmp[:, 1], in0=tmp[:, 2], scalar=-C3, in1=tmp[:, 1], op0=M,
                                           op1=AD).then_inc(dve_order, 1)
                    dve.wait_ge(dve_order, counted(dve_order))
                    if r > 0:
                        dve.wait_ge(sin_ready, r)
                    v.tensor_scalar(scr[:, 4], tmp[:, 1], quarter * TWO_PI, PI_SAFE, AD, MN).then_inc(dve_order, 1)
                    dve.wait_ge(dve_order, counted(dve_order))
                    v.tensor_scalar(scr[:, 4], scr[:, 4], -PI_SAFE, None, MX).then_inc(angle_ready, 1)
                    dve.wait_ge(angle_ready, counted(angle_ready))

            norm_apply(1, lambda k: sm(A2 + k), shift=lambda k: sm(MOD + 24 + k))
            for t in range(THIRDS):
                for c in range(8 * t, 8 * t + 8):
                    b = c % 2
                    for half, o, started, done in ((0, scr[:, b], convg_started, convg_done),
                                                   (24, scr[:, 2 + b], convv_started, convv_done)):
                        n = UNIT[("ff_g" if half == 0 else "ff_v", c)]
                        dve.wait_ge(started, c + 1)
                        for s in (1, 2):
                            signal = done if s == 2 else dve_order
                            v.scalar_tensor_tensor(out=o[:, s:T], in0=psum_of(n)[:, 0:T - s],
                                                   scalar=p_("ffn_conv_w", 48 * (2 - s) + half + c), in1=o[:, s:T], op0=M, op1=AD)\
                                .then_inc(signal, 1)
                            dve.wait_ge(signal, counted(signal))
                    dve.wait_ge(ffgelu_done, c + 1)
                    v.tensor_tensor(tmp[:, 0], scr[:, b], scr[:, 2 + b], M).then_inc(dve_order, 1)
                    dve.wait_ge(dve_order, counted(dve_order))
                    if c % 8 == 0 and t:
                        dve.wait_ge(unit_done, UNIT[("ff_down", 8 * t - 1)] + 1)
                    v.tensor_copy(y_hi[:, c % 8], tmp[:, 0]).then_inc(dve_order, 1)
                    dve.wait_ge(dve_order, counted(dve_order))
                    v.tensor_tensor(y_lo[:, c % 8], tmp[:, 0], y_hi[:, c % 8].bitcast(F32), SU).then_inc(ff_ready, 1)
                    dve.wait_ge(ff_ready, counted(ff_ready))
                    if 2 <= c < 14:
                        angle((c - 2) // 3, (c - 2) % 3)
                for m in range(8):
                    n = UNIT[("ff_down", 8 * t + m)]
                    dve.wait_ge(unit_done, n + 1)
                    v.scalar_tensor_tensor(out=x[:, m], in0=psum_of(n), scalar=sm(MOD + 40 + m), in1=x[:, m],
                                           op0=M, op1=AD).then_inc(resf_done, 1)
                    dve.wait_ge(resf_done, counted(resf_done))
            norm_apply(2, lambda k: p_("a_norm_g", k))
            def rotate(x1, x2, sin, cos, done):
                v.tensor_tensor(ksr[:, 0], x1, sin, M).then_inc(dve_order, 1)
                dve.wait_ge(dve_order, counted(dve_order))
                v.tensor_tensor(ksr[:, 1], x2, sin, M).then_inc(dve_order, 1)
                dve.wait_ge(dve_order, counted(dve_order))
                v.tensor_tensor(x1, x1, cos, M).then_inc(dve_order, 1)
                dve.wait_ge(dve_order, counted(dve_order))
                v.tensor_tensor(x1, x1, ksr[:, 1], SU).then_inc(dve_order, 1)
                dve.wait_ge(dve_order, counted(dve_order))
                v.tensor_tensor(x2, x2, cos, M).then_inc(dve_order, 1)
                dve.wait_ge(dve_order, counted(dve_order))
                v.tensor_tensor(x2, x2, ksr[:, 0], AD).then_inc(done, 1)
                dve.wait_ge(done, counted(done))

            dve.wait_ge(inv_loaded, 16)
            v.memset(u_pad, 0.0).then_inc(pad_set, 1)
            dve.wait_ge(pad_set, counted(pad_set))

            def rotate_stacked(out, kind, j, read):
                n = UNIT[(kind, j)]
                dve.wait_ge(unit_done, n + 1)
                v.tensor_tensor(out, psum_of(n), rope[:, 1], M).then_inc(read, 1)
                dve.wait_ge(read, counted(read))
                dve.wait_ge(unit_done, n + 2)
                v.tensor_tensor(tmp[:, 3], psum_of(n + 1), rope[:, 0], M).then_inc(read, 1)
                dve.wait_ge(read, counted(read))
                v.tensor_tensor(out, out, tmp[:, 3], AD).then_inc(ropes_done, 1)
                dve.wait_ge(ropes_done, counted(ropes_done))

            rotate_stacked(krr, "kr", 0, kr_read)
            for g in range(5):
                if g == 0:
                    dve.wait_ge(norm_rooted, 4)
                    for j in range(3):
                        v.scalar_tensor_tensor(out=tmp[:, j], in0=cq_sb[:, j], scalar=p_("a_q_norm_g", j),
                                               in1=rstd[:], op0=M, op1=M).then_inc(pre_c, 1)
                        dve.wait_ge(pre_c, counted(pre_c))
                        dve.wait_ge(c_high, j + 1)
                        v.tensor_tensor(cq_lo[:, j], tmp[:, j], cq_hi[:, j].bitcast(F32), SU).then_inc(cqn_ready, 1)
                        dve.wait_ge(cqn_ready, counted(cqn_ready))
                for c in (2 * g, 2 * g + 1):
                    if g > 0:
                        dve.wait_ge(unit_done, UNIT[("pool", c - 2)] + 1)
                        v.scalar_tensor_tensor(out=tmp[:, c % 2], in0=psum_of(UNIT[("pool", c - 2)]),
                                               scalar=p_("a_pool_scale", c - 2), in1=sg_p[:, c % 2], op0=M, op1=M)\
                            .then_inc(pool_done, 1)
                        dve.wait_ge(pool_done, counted(pool_done))
                    if g < 4:
                        dve.wait_ge(u_copied, c + 1)
                        src, wlen = u_pad[:, c % 2], T + 16
                        for d in range(g + 1):
                            wlen -= 2 ** d
                            dst = win[:, d % 2]
                            v.tensor_tensor(dst[:, 0:wlen], src[:, 0:wlen], src[:, 2 ** d:2 ** d + wlen],
                                            AD).then_inc(dve_order, 1)
                            dve.wait_ge(dve_order, counted(dve_order))
                            src = dst
                        left = 8 - 2 ** g
                        v.tensor_tensor(tmp[:, 2], src[:, left:left + T], inv_count[:, g], M).then_inc(dve_order, 1)
                        dve.wait_ge(dve_order, counted(dve_order))
                        v.tensor_tensor(tmp[:, 2], tmp[:, 2], u_pad[:, c % 2, 8:8 + T], SU).then_inc(dve_order, 1)
                        dve.wait_ge(dve_order, counted(dve_order))
                        v.tensor_copy(y_hi[:, c], tmp[:, 2]).then_inc(dve_order, 1)
                        dve.wait_ge(dve_order, counted(dve_order))
                        v.tensor_tensor(y_lo[:, c], tmp[:, 2], y_hi[:, c].bitcast(F32), SU).then_inc(d_ready, 1)
                        dve.wait_ge(d_ready, counted(d_ready))
                if g > 0:
                    for c in (2 * g - 2, 2 * g - 1):
                        dve.wait_ge(yp_high, c + 1)
                        v.tensor_tensor(y_lo[:, c], tmp[:, c % 2], y_hi[:, c].bitcast(F32), SU).then_inc(yp_ready, 1)
                        dve.wait_ge(yp_ready, counted(yp_ready))
                if g == 0:
                    dve.wait_ge(norm_rooted, 5)
                    v.scalar_tensor_tensor(out=tmp[:, 3], in0=cq_sb[:, 3], scalar=p_("a_kv_norm_g"),
                                           in1=rstd[:], op0=M, op1=M).then_inc(pre_c, 1)
                    dve.wait_ge(pre_c, counted(pre_c))
                    dve.wait_ge(c_high, 4)
                    v.tensor_tensor(cq_lo[:, 3], tmp[:, 3], cq_hi[:, 3].bitcast(F32), SU).then_inc(cqn_ready, 1)
                    dve.wait_ge(cqn_ready, counted(cqn_ready))
            for m in range(8):
                n = UNIT[("p_out", m)]
                dve.wait_ge(unit_done, n + 1)
                v.tensor_tensor(x[:, m], psum_of(n), x[:, m], AD).then_inc(resp_done, 1)
                dve.wait_ge(resp_done, counted(resp_done))
            for j in range(4):
                rotate_stacked(qrr[:, j], "qr", 2 * j, qr_read)
            dve.wait_ge(unit_done, UNIT[("p_out", 7)] + 1)
            for h in range(HEADS + 1):
                g = h - 1
                if h < HEADS:
                    for b in range(TB + 1):
                        q = 4 * h + b
                        if b < TB:
                            dve.wait_ge(s_done, q + 1)
                            v.reduce_max(sm(STAT + 8), big[:, q % 3], AX_X).then_inc(dve_order, 1)
                            dve.wait_ge(dve_order, counted(dve_order))
                            v.tensor_scalar(sm(STAT + b), sm(STAT + 8), -(192.0 ** -0.5), None,
                                            M).then_inc(max_done, 1)
                            dve.wait_ge(max_done, counted(max_done))
                        if b > 0:
                            dve.wait_ge(p_exp, q)
                            v.reciprocal(sm(STAT + 3 + b), sm(STAT + 3 + b)).then_inc(dve_order, 1)
                            dve.wait_ge(dve_order, counted(dve_order))
                            v.tensor_scalar(p_sb[:, b - 1], p_sb[:, b - 1], sm(STAT + 3 + b), None,
                                            M).then_inc(p_ready, 1)
                            dve.wait_ge(p_ready, counted(p_ready))
                if g >= 0:
                    dve.wait_ge(pv_done, g + 1)
                    dve.wait_ge(agate_done, g + 1)
                    v.tensor_tensor(tmp[:, 0], m_o[:], sg_a[:, g % 2], M).then_inc(dve_order, 1)
                    dve.wait_ge(dve_order, counted(dve_order))
                    v.tensor_copy(y_hi[:, g], tmp[:, 0]).then_inc(dve_order, 1)
                    dve.wait_ge(dve_order, counted(dve_order))
                    v.tensor_tensor(y_lo[:, g], tmp[:, 0], y_hi[:, g].bitcast(F32), SU).then_inc(ya_ready, 1)
                    dve.wait_ge(ya_ready, counted(ya_ready))
            for m in range(8):
                n = UNIT[("a_out", m)]
                dve.wait_ge(unit_done, n + 1)
                v.tensor_tensor(x[:, m], psum_of(n), x[:, m], AD).then_inc(resa_done, 1)
                dve.wait_ge(resa_done, counted(resa_done))
            norm_apply(3, lambda k: p_("r_norm_g", k))
            df = c_("diff")
            for h in range(RH):
                if 4 * h > 0:
                    dve.wait_ge(rs_done, 4 * h)
                W = T + 3 * P
                tw = s_sb[:, 0:2].rearrange("p a t -> p (a t)")[:, 0:W]
                v.tensor_scalar(dtab, df, 0.0, sm(LOGG + h), MX, M).then_inc(dve_order, 1)
                dve.wait_ge(dve_order, counted(dve_order))
                v.tensor_scalar(tw, df, 0.0, sm(LOGG + 4 + h), MN, M).then_inc(dve_order, 1)
                dve.wait_ge(dve_order, counted(dve_order))
                v.tensor_tensor(dtab, dtab, tw, SU).then_inc(dlog_done, 1)
                dve.wait_ge(dlog_done, counted(dlog_done))
                dve.wait_ge(rq_copied, 2 * h + 2)
                rotate(rq_r[:, 0], rq_r[:, 1], rope[:, 2], rope[:, 3], rope_done)
                dve.wait_ge(rk_copied, 2 * h + 2)
                rotate(rk_r[:, 0], rk_r[:, 1], rope[:, 2], rope[:, 3], rope_done)
                dve.wait_ge(dexp_done, h + 1)
                for j in range(TB):
                    dve.wait_ge(rs_scores, 4 * h + j + 1)
                    v.scalar_tensor_tensor(out=s_sb[:, j], in0=big[:, (4 * h + j) % 3],
                                           scalar=float(RDK) ** -0.5, in1=dtab[:, (3 - j) * P:(3 - j) * P + T], op0=M, op1=M)\
                        .then_inc(rs_done, 1)
                    dve.wait_ge(rs_done, counted(rs_done))
                for b in range(TB):
                    dve.wait_ge(ro_done, 4 * h + b + 1)
                    v.bn_stats(sm(STAT + 10, 6), ro_bank[b]).then_inc(dve_order, 1)
                    dve.wait_ge(dve_order, counted(dve_order))
                    v.bn_aggr(sm(STAT + 8, 2), sm(STAT + 10, 6)).then_inc(var_done, 1)
                    dve.wait_ge(var_done, counted(var_done))
                    dve.wait_ge(vroot_done, 4 * h + b + 1)
                    v.reciprocal(sm(STAT + 17), sm(STAT + 16)).then_inc(dve_order, 1)
                    dve.wait_ge(dve_order, counted(dve_order))
                    v.scalar_tensor_tensor(out=sm(STAT + 18), in0=sm(STAT + 8), scalar=-1.0, in1=sm(STAT + 17),
                                           op0=M, op1=M).then_inc(nmu_done, 1)
                    dve.wait_ge(nmu_done, counted(nmu_done))
                    dve.wait_ge(on_done, 4 * h + b + 1)
                dve.wait_ge(rgate_done, 4 * h + 4)
                for c in range(4):
                    dve.wait_ge(ont_done, 4 * h + c + 1)
                    v.scalar_tensor_tensor(out=tmp[:, c % 2], in0=ont_bank[c], scalar=p_("r_gn_g", 4 * h + c),
                                           in1=sg_r[:, c], op0=M, op1=M).then_inc(yrp_done, 1)
                    dve.wait_ge(yrp_done, counted(yrp_done))
                    dve.wait_ge(yr_high, 4 * h + c + 1)
                    kk = 4 * (h % 2) + c
                    v.tensor_tensor(y_lo[:, kk], tmp[:, c % 2], y_hi[:, kk].bitcast(F32), SU).then_inc(yr_ready, 1)
                    dve.wait_ge(yr_ready, counted(yr_ready))
                if h % 2:
                    for m in range(8):
                        n = UNIT[("r_out", 8 * (h // 2) + m)]
                        dve.wait_ge(unit_done, n + 1)
                        v.tensor_tensor(x[:, m], psum_of(n), x[:, m], AD).then_inc(resr_done, 1)
                        dve.wait_ge(resr_done, counted(resr_done))
            dve.wait_ge(norm_rooted, 7)
            for k in range(DK):
                v.scalar_tensor_tensor(out=scr[:, k], in0=x[:, k], scalar=p_("final_norm_g", k), in1=rstd[:],
                                       op0=M, op1=M).then_inc(out_ready, 1)
                dve.wait_ge(out_ready, counted(out_ready))


def constants():
    c = np.zeros((P, NCONST), np.float32)

    def put(name, a):
        at, n = CONST[name]
        c[:, at:at + n] = a
    p = np.arange(P)[:, None]
    f = np.arange(P)[None, :]
    put("ident", p == f)
    put("later_ones", np.concatenate([p > f, np.ones((P, P), bool)], axis=1))
    put("ones", 1.0)
    put("mask", p < f)
    put("diff", np.arange(T + 3 * P)[None, :] - 3 * P - p)
    put("freq_a", np.where(p % 64 < 32, -1.0, 1.0) / 10000.0 ** ((p % 32) * 2 / 64))
    put("freq_r", 1.0 / 10000.0 ** (np.arange(P)[:, None] * 2 / 256))
    return c


def inverse_counts():
    t = np.arange(T)
    inv = []
    for w in (2, 4, 8, 16):
        lo = np.clip(t - w // 2, 0, T - 1)
        hi = np.clip(t + w // 2 - 1, 0, T - 1)
        inv.append(1.0 / (hi - lo + 1))
    return np.ascontiguousarray(np.broadcast_to(np.stack(inv).astype(np.float32), (P, 4, T)))


def columns(a):
    return np.asarray(a).reshape(-1, P).T


def blocks(w):
    k = w.shape[0] // P
    return w.reshape(k, P, P).transpose(1, 0, 2).reshape(P, k * P)


def kernel(**inputs):
    import concourse.bacc as _bacc
    from concourse.bass_utils import run_bass_kernel_spmd as _run

    i = {k: np.asarray(v) for k, v in inputs.items()}
    w_in, up = i["w_in"][0], i["ffn_up"][0]
    a_in, uq, ukv = i["a_w_in_2"][0], i["a_w_uq_2"][0], i["a_w_ukv_2"][0]
    a_out, r_in, r_out = i["a_w_out_2"][0], i["r_w_in_2"][0], i["r_w_out_2"][0]
    U0 = 384 + 128 + 64
    G0 = U0 + 1024

    def cut(w, j):
        return w[:, j * P:(j + 1) * P]

    def source(kind, j):
        part = {"xr": 0, "yr": 1, "q": 2, "k": 3, "v": 4, "ga": 5, "gb": 6}
        if kind in part:
            return cut(w_in, 8 * part[kind] + j)
        if kind == "w_out":
            return cut(i["w_out"][0], j)
        if kind == "ff_g":
            return cut(up, j)
        if kind == "ff_v":
            return cut(up, 24 + j)
        if kind == "ff_down":
            return cut(i["ffn_down"][0][D * (j // 8):D * (j // 8 + 1)], j % 8)
        if kind == "cq":
            return cut(a_in, j)
        if kind == "ckv":
            return cut(a_in, 3)
        if kind == "kr":
            halves = a_in[:, 512:576].reshape(D, 2, 32)
            return np.tile(halves[:, ::1 - 2 * j].reshape(D, 64), (1, 2))
        if kind == "u":
            return cut(a_in[:, U0:], j)
        if kind == "pgate":
            return cut(a_in[:, G0 + 1024:], j)
        if kind == "agate":
            return cut(a_in[:, G0:], j)
        if kind == "pool":
            return cut(i["a_pool_w_2"][0, j // 2], j % 2)
        if kind == "p_out":
            return cut(a_out[D:], j)
        if kind == "a_out":
            return cut(a_out[:D], j)
        if kind == "qr":
            halves = uq.reshape(384, 8, 192)[:, 2 * (j // 2):2 * (j // 2) + 2, 128:].reshape(384, 2, 2, 32)
            return halves[:, :, ::1 - 2 * (j % 2)].reshape(384, P)
        if kind == "qn":
            return uq[:, 192 * j:192 * j + P]
        if kind == "kn":
            return ukv[:, 256 * j:256 * j + P]
        if kind == "vn":
            return ukv[:, 256 * j + P:256 * j + 2 * P]
        at = {"rq": 0, "rk": 8, "rv": 16, "rgate": 32}
        if kind in at:
            return cut(r_in, at[kind] + j)
        return cut(r_out[D * (j // 8):D * (j // 8 + 1)], j % 8)

    weights = np.zeros((NU, P, 8 * P), np.float32)
    for n, (kind, j, nk) in enumerate(UNITS):
        weights[n, :, :nk * P] = blocks(source(kind, j))
    ada = i["ada_w"][0].reshape(DK, P, 6, D).transpose(1, 2, 0, 3).reshape(P, NADA, 2, T)
    params = np.concatenate([
        columns(i["c"]), columns(i["ada_b"]), columns(i["norm1_g"]), columns(i["conv_w"]),
        columns(i["conv_b"]), columns(i["rg_ba"]), columns(i["rg_bx"]), columns(i["rg_lambda"]),
        np.tile(i["r_decay_fwd_2"], (P, 1)), np.tile(i["r_decay_bwd_2"], (P, 1)),
        columns(i["q_norm_g"]), columns(i["k_norm_g"]), columns(i["norm2_g"]), columns(i["ffn_conv_w"]),
        columns(i["ffn_conv_b"]), columns(i["a_norm_g_2"]), columns(i["a_q_norm_g_2"]),
        columns(i["a_kv_norm_g_2"]), columns(i["a_pool_scale_2"]), columns(i["r_norm_g_2"]),
        columns(i["r_gn_g_2"]), columns(i["final_norm_g_2"])], axis=1)
    arrays = {
        "ada": np.ascontiguousarray(ada),
        "weights": weights,
        "params": np.ascontiguousarray(params),
        "consts": constants(),
        "rg_w": np.ascontiguousarray(np.concatenate([i["rg_wa"][0], i["rg_wx"][0]]).transpose(1, 0, 2)),
        "x_t": np.ascontiguousarray(i["x"][0].T.reshape(DK, P, T).transpose(1, 0, 2)),
        "positions": np.ascontiguousarray(i["positions_2"].reshape(1, T).repeat(P, 0)),
        "inv_counts": inverse_counts(),
    }
    nc = _bacc.Bacc("TRN2", target_bir_lowering=False, num_devices=1, dynamic_dma_scratch_size=1024)
    aps = [nc.dram_tensor(n, a.shape, mybir.dt.from_np(a.dtype), kind="ExternalInput").ap()
           for n, a in arrays.items()]
    out_t = nc.dram_tensor("out_t", [P, DK, T], F32, kind="ExternalOutput").ap()
    build(nc, *aps, out_t)
    r = _run(nc, [arrays], core_ids=[0])
    got = r.results[0]["out_t"]
    return np.ascontiguousarray(got.transpose(1, 0, 2).reshape(D, T).T).reshape(1, T, D)
```
